# Optimizing a Trainium2 kernel written in Bass

```python
import jax, jax.numpy as jnp
from jax import lax
import numpy as np
import math

D_MODEL = 2048
BATCH = 1
SEQ = 256
DEPTH = 1

CHUNK = 64
Q_BLOCK = 128
N_BRANCH = 3
D_RNN = D_MODEL // 2
N_RNN_BLOCKS = 8
RNN_BLOCK = D_RNN // N_RNN_BLOCKS
CONV_WIDTH = 4
LRU_C = 8.0
N_HEADS = 8
HEAD_DIM = 128
D_ATTN = N_HEADS * HEAD_DIM
D_POOL = D_MODEL // 2
POOL_WINDOWS = (2, 4, 8, 16)
N_POOL_GROUPS = 4
POOL_GROUP = D_POOL // N_POOL_GROUPS
D_FF = ((-(-8 * D_MODEL // 3) + 255) // 256) * 256
NORM_EPS = 1e-6
IN_SIZES = (D_RNN, D_RNN, D_ATTN, D_ATTN, D_ATTN, N_HEADS, D_POOL, N_BRANCH * D_MODEL)
D_IN = D_RNN * 2 + D_ATTN * 3 + N_HEADS + D_POOL + N_BRANCH * D_MODEL


def rms_norm(x, g):
    xf = x.astype(jnp.float32)
    y = xf * lax.rsqrt(jnp.mean(xf * xf, axis=-1, keepdims=True) + NORM_EPS)
    return (y * g.astype(jnp.float32)).astype(x.dtype)

def split_columns(p):
    offsets = []
    acc = 0
    for s in IN_SIZES[:-1]:
        acc += s
        offsets.append(acc)
    return jnp.split(p, offsets, axis=-1)

def causal_depthwise_conv(u, w, b):
    S = u.shape[1]
    up = jnp.pad(u, ((0, 0), (CONV_WIDTH - 1, 0), (0, 0)))
    out = b + up[:, 0:S] * w[0]
    for k in range(1, CONV_WIDTH):
        out = out + up[:, k:k + S] * w[k]
    return out

def rg_lru(u, w_r, b_r, w_i, b_i, lam):
    B, S, _ = u.shape
    ub = u.reshape(B, S, N_RNN_BLOCKS, RNN_BLOCK)
    r = jax.nn.sigmoid(jnp.einsum('bsnc,ncd->bsnd', ub, w_r).reshape(B, S, D_RNN) + b_r)
    i = jax.nn.sigmoid(jnp.einsum('bsnc,ncd->bsnd', ub, w_i).reshape(B, S, D_RNN) + b_i)
    log_a = (LRU_C * r.astype(jnp.float32)) * jax.nn.log_sigmoid(lam.astype(jnp.float32))
    a = jnp.exp(log_a)
    b_in = jnp.sqrt(-jnp.expm1(2.0 * log_a)) * (i * u).astype(jnp.float32)

    def combine(left, right):
        a1, b1 = left
        a2, b2 = right
        return a1 * a2, a2 * b1 + b2

    _, h = lax.associative_scan(combine, (a, b_in), axis=1)
    return h.astype(u.dtype)

def forgetting_attention(q, k, v, f_logit):
    B, S, H, Dh = q.shape
    nb = S // Q_BLOCK
    scale = Dh ** -0.5
    F = jnp.cumsum(jax.nn.log_sigmoid(f_logit.astype(jnp.float32)), axis=1).transpose(0, 2, 1)
    k_h = k.transpose(0, 2, 1, 3)
    v_h = v.transpose(0, 2, 1, 3)
    q_blocks = q.reshape(B, nb, Q_BLOCK, H, Dh).transpose(1, 0, 3, 2, 4)
    F_blocks = F.reshape(B, H, nb, Q_BLOCK).transpose(2, 0, 1, 3)
    k_pos = jnp.arange(S)

    def one_block(args):
        qb, Fq, blk = args
        s = jnp.einsum('bhqd,bhkd->bhqk', qb, k_h, preferred_element_type=jnp.float32) * scale
        s = s + Fq[..., None] - F[:, :, None, :]
        q_pos = blk * Q_BLOCK + jnp.arange(Q_BLOCK)
        s = jnp.where(q_pos[:, None] >= k_pos[None, :], s, -jnp.inf)
        p = jax.nn.softmax(s, axis=-1)
        return jnp.einsum('bhqk,bhkd->bhqd', p.astype(v_h.dtype), v_h)

    o = lax.map(one_block, (q_blocks, F_blocks, jnp.arange(nb)))
    return o.transpose(1, 0, 3, 2, 4).reshape(B, S, H * Dh)

def multiscale_pool(u, w_pool, scale):
    B, S, _ = u.shape
    uf = u.astype(jnp.float32).reshape(B, S, N_POOL_GROUPS, POOL_GROUP)
    cs = jnp.cumsum(uf, axis=1)
    t = jnp.arange(1, S + 1, dtype=jnp.float32)
    outs = []
    for g, w in enumerate(POOL_WINDOWS):
        c = cs[:, :, g]
        lagged = jnp.pad(c, ((0, 0), (w, 0), (0, 0)))[:, :S]
        cnt = jnp.minimum(t, w)[None, :, None]
        outs.append((c - lagged) / cnt - uf[:, :, g])
    pooled = jnp.stack(outs, axis=2).astype(u.dtype)
    y = jnp.einsum('bsgc,gcd->bsgd', pooled, w_pool).reshape(B, S, D_POOL)
    return y * scale

def hybrid_layer(x, g_mix, w_in, b_forget, conv_w, conv_b, w_rg, b_rg, w_ig, b_ig, lru_lambda,
                 w_pool, pool_scale, w_branch_rnn, w_branch_attn, w_branch_pool, w_out,
                 g_ffn, w_ffn_in, w_ffn_out):
    B, S, _ = x.shape
    h = rms_norm(x, g_mix)
    rnn_x, rnn_y, q, k, v, f_logit, pool_in, gate_logits = split_columns(h @ w_in)
    u = causal_depthwise_conv(rnn_x, conv_w, conv_b)
    y_a = jax.nn.gelu(rnn_y) * rg_lru(u, w_rg, b_rg, w_ig, b_ig, lru_lambda)
    y_b = forgetting_attention(q.reshape(B, S, N_HEADS, HEAD_DIM),
                               k.reshape(B, S, N_HEADS, HEAD_DIM),
                               v.reshape(B, S, N_HEADS, HEAD_DIM),
                               f_logit + b_forget)
    y_c = multiscale_pool(pool_in, w_pool, pool_scale)
    gates = jax.nn.sigmoid(gate_logits.astype(jnp.float32)).astype(x.dtype).reshape(B, S, N_BRANCH, D_MODEL)
    merged = (gates[:, :, 0] * (y_a @ w_branch_rnn)
              + gates[:, :, 1] * (y_b @ w_branch_attn)
              + gates[:, :, 2] * (y_c @ w_branch_pool))
    x = x + merged @ w_out
    h2 = rms_norm(x, g_ffn)
    gate, up = jnp.split(h2 @ w_ffn_in, 2, axis=-1)
    return x + (jax.nn.silu(gate) * up) @ w_ffn_out

def first_inputs(seed: int = 0) -> dict:
    key = jax.random.key(seed)
    ks = jax.random.split(key, 24)
    f32 = jnp.float32
    nrm = lambda k, shape, s: jax.random.normal(k, shape, f32) * s
    a8 = jax.random.uniform(ks[10], (DEPTH, D_RNN), f32, 0.9, 0.999)
    a = a8 ** (1.0 / LRU_C)
    lru_lambda = jnp.log(a) - jnp.log1p(-a)
    return {
        "x": jax.random.normal(ks[0], (BATCH, SEQ, D_MODEL), f32),
        "g_mix": 1.0 + nrm(ks[1], (DEPTH, D_MODEL), 0.05),
        "w_in": nrm(ks[2], (DEPTH, D_MODEL, D_IN), D_MODEL ** -0.5),
        "b_forget": jax.random.uniform(ks[3], (DEPTH, N_HEADS), f32, 1.0, 4.0),
        "conv_w": nrm(ks[4], (DEPTH, CONV_WIDTH, D_RNN), CONV_WIDTH ** -0.5),
        "conv_b": nrm(ks[5], (DEPTH, D_RNN), 0.02),
        "w_rg": nrm(ks[6], (DEPTH, N_RNN_BLOCKS, RNN_BLOCK, RNN_BLOCK), RNN_BLOCK ** -0.5),
        "b_rg": nrm(ks[7], (DEPTH, D_RNN), 0.02),
        "w_ig": nrm(ks[8], (DEPTH, N_RNN_BLOCKS, RNN_BLOCK, RNN_BLOCK), RNN_BLOCK ** -0.5),
        "b_ig": nrm(ks[9], (DEPTH, D_RNN), 0.02),
        "lru_lambda": lru_lambda,
        "w_pool": nrm(ks[11], (DEPTH, N_POOL_GROUPS, POOL_GROUP, POOL_GROUP), POOL_GROUP ** -0.5),
        "pool_scale": 1.0 + nrm(ks[12], (DEPTH, D_POOL), 0.1),
        "w_branch_rnn": nrm(ks[13], (DEPTH, D_RNN, D_MODEL), D_RNN ** -0.5),
        "w_branch_attn": nrm(ks[14], (DEPTH, D_ATTN, D_MODEL), D_ATTN ** -0.5),
        "w_branch_pool": nrm(ks[15], (DEPTH, D_POOL, D_MODEL), D_POOL ** -0.5),
        "w_out": nrm(ks[16], (DEPTH, D_MODEL, D_MODEL), D_MODEL ** -0.5),
        "g_ffn": 1.0 + nrm(ks[17], (DEPTH, D_MODEL), 0.05),
        "w_ffn_in": nrm(ks[18], (DEPTH, D_MODEL, 2 * D_FF), D_MODEL ** -0.5),
        "w_ffn_out": nrm(ks[19], (DEPTH, D_FF, D_MODEL), D_FF ** -0.5),
        "g_final": 1.0 + nrm(ks[20], (D_MODEL,), 0.05),
    }

def first_block(x, g_mix, w_in, b_forget, conv_w, conv_b, w_rg, b_rg, w_ig, b_ig, lru_lambda,
              w_pool, pool_scale, w_branch_rnn, w_branch_attn, w_branch_pool, w_out,
              g_ffn, w_ffn_in, w_ffn_out, g_final):
    for l in range(DEPTH):
        x = hybrid_layer(x, g_mix[l], w_in[l], b_forget[l], conv_w[l], conv_b[l], w_rg[l], b_rg[l],
                         w_ig[l], b_ig[l], lru_lambda[l], w_pool[l], pool_scale[l],
                         w_branch_rnn[l], w_branch_attn[l], w_branch_pool[l], w_out[l],
                         g_ffn[l], w_ffn_in[l], w_ffn_out[l])
    return rms_norm(x, g_final)


GRID_W = 64
A_Q_HEADS = 8
A_KV_HEADS = 2
A_GROUP = A_Q_HEADS // A_KV_HEADS
B_HEADS = 8
WIN_ROWS_MAX = 8
WIN_COLS = 16
A_WIDTH = A_Q_HEADS * HEAD_DIM
B_WIDTH = B_HEADS * HEAD_DIM
MIX_WIDTH = A_WIDTH + B_WIDTH
A_KV_WIDTH = A_KV_HEADS * HEAD_DIM
IN_WIDTH = A_WIDTH + 2 * A_KV_WIDTH + 3 * B_WIDTH
D_FF_2 = 4 * D_MODEL
PLE_DIM = 256
ROPE_THETA = 10000.0
ROPE_AXIS_DIM = HEAD_DIM // 2


def rms_norm_2(x, g):
    xf = x.astype(jnp.float32)
    y = xf * lax.rsqrt(jnp.mean(xf * xf, axis=-1, keepdims=True) + NORM_EPS)
    return (y * g.astype(jnp.float32)).astype(x.dtype)

def rope_half(x, ang):
    n = ang.shape[-1]
    shape = (1, ang.shape[0]) + (1,) * (x.ndim - 3) + (n,)
    cos = jnp.cos(ang).reshape(shape)
    sin = jnp.sin(ang).reshape(shape)
    xf = x.astype(jnp.float32)
    x1, x2 = xf[..., :n], xf[..., n:]
    return jnp.concatenate([x1 * cos - x2 * sin, x2 * cos + x1 * sin], axis=-1).astype(x.dtype)

def axial_rope(x, ang_row, ang_col):
    return jnp.concatenate([rope_half(x[..., :ROPE_AXIS_DIM], ang_row),
                            rope_half(x[..., ROPE_AXIS_DIM:], ang_col)], axis=-1)

def to_blocks(a):
    b, s = a.shape[0], a.shape[1]
    a = a.reshape((b, s // Q_BLOCK, Q_BLOCK) + a.shape[2:])
    return jnp.moveaxis(a, 1, 0)

def from_blocks(a):
    a = jnp.moveaxis(a, 0, 1)
    return a.reshape((a.shape[0], a.shape[1] * a.shape[2]) + a.shape[3:])

def global_gqa(q, k, v):
    scale = 1.0 / math.sqrt(HEAD_DIM)

    def block(qb):
        s = jnp.einsum('bqkgd,bskd->bkgqs', qb, k).astype(jnp.float32) * scale
        w = jax.nn.softmax(s, axis=-1).astype(v.dtype)
        return jnp.einsum('bkgqs,bskd->bqkgd', w, v)

    o = lax.map(block, to_blocks(q))
    return from_blocks(o)

def neighbourhood_attn(q, k, v, rpb, rows):
    s_len = q.shape[1]
    win_r = min(WIN_ROWS_MAX, rows)
    scale = 1.0 / math.sqrt(HEAD_DIM)
    t_blocks = jnp.arange(s_len, dtype=jnp.int32).reshape(s_len // Q_BLOCK, Q_BLOCK)
    ar_r = jnp.arange(win_r, dtype=jnp.int32)
    ar_c = jnp.arange(WIN_COLS, dtype=jnp.int32)

    def block(args):
        qb, t = args
        r = t // GRID_W
        c = t % GRID_W
        r0 = jnp.clip(r - win_r // 2, 0, rows - win_r)
        c0 = jnp.clip(c - WIN_COLS // 2, 0, GRID_W - WIN_COLS)
        kr = r0[:, None] + ar_r[None, :]
        kc = c0[:, None] + ar_c[None, :]
        idx = (kr[:, :, None] * GRID_W + kc[:, None, :]).reshape(Q_BLOCK, win_r * WIN_COLS)
        dr = kr - r[:, None] + (WIN_ROWS_MAX - 1)
        dc = kc - c[:, None] + (WIN_COLS - 1)
        bias = rpb[:, dr[:, :, None], dc[:, None, :]].reshape(B_HEADS, Q_BLOCK, win_r * WIN_COLS)
        kg = k[:, idx]
        vg = v[:, idx]
        s = jnp.einsum('bqhd,bqnhd->bhqn', qb, kg).astype(jnp.float32) * scale
        s = s + bias.astype(jnp.float32)[None]
        w = jax.nn.softmax(s, axis=-1).astype(vg.dtype)
        return jnp.einsum('bhqn,bqnhd->bqhd', w, vg)

    o = lax.map(block, (to_blocks(q), t_blocks))
    return from_blocks(o)

def second_inputs(seed: int = 0) -> dict:
    key = jax.random.key(seed)
    ks = jax.random.split(key, 20)
    f32 = jnp.float32

    def w(k, shape, fan_in):
        return jax.random.normal(k, shape, f32) * (fan_in ** -0.5)

    def gain(k, shape):
        return 1.0 + 0.05 * jax.random.normal(k, shape, f32)

    return {
        "x": jax.random.normal(ks[0], (BATCH, SEQ, D_MODEL), f32),
        "p": jax.random.normal(ks[1], (DEPTH, BATCH, SEQ, PLE_DIM), f32),
        "pre_mix_norm": gain(ks[2], (DEPTH, D_MODEL)),
        "w_in": w(ks[3], (DEPTH, D_MODEL, IN_WIDTH), D_MODEL),
        "q_norm": gain(ks[4], (DEPTH, HEAD_DIM)),
        "k_norm": gain(ks[5], (DEPTH, HEAD_DIM)),
        "rel_pos_bias": 0.1 * jax.random.normal(ks[6], (DEPTH, B_HEADS, 2 * WIN_ROWS_MAX - 1, 2 * WIN_COLS - 1), f32),
        "w_o": w(ks[7], (DEPTH, MIX_WIDTH, D_MODEL), MIX_WIDTH),
        "post_mix_norm": gain(ks[8], (DEPTH, D_MODEL)),
        "pre_mlp_norm": gain(ks[9], (DEPTH, D_MODEL)),
        "w_up": w(ks[10], (DEPTH, D_MODEL, D_FF_2), D_MODEL),
        "w_down": w(ks[11], (DEPTH, D_FF_2, D_MODEL), D_FF_2),
        "post_mlp_norm": gain(ks[12], (DEPTH, D_MODEL)),
        "pre_ple_norm": gain(ks[13], (DEPTH, D_MODEL)),
        "w_ple_gate": w(ks[14], (DEPTH, D_MODEL, D_MODEL), D_MODEL),
        "w_ple_proj": w(ks[15], (DEPTH, PLE_DIM, D_MODEL), PLE_DIM),
        "post_ple_norm": gain(ks[16], (DEPTH, D_MODEL)),
    }

def second_block(x, p, pre_mix_norm, w_in, q_norm, k_norm, rel_pos_bias, w_o, post_mix_norm,
              pre_mlp_norm, w_up, w_down, post_mlp_norm, pre_ple_norm, w_ple_gate, w_ple_proj,
              post_ple_norm):
    b, s_len, _ = x.shape
    rows = s_len // GRID_W
    t = jnp.arange(s_len, dtype=jnp.int32)
    row = (t // GRID_W).astype(jnp.float32)
    col = (t % GRID_W).astype(jnp.float32)
    n_freq = ROPE_AXIS_DIM // 2
    freqs = ROPE_THETA ** (-jnp.arange(n_freq, dtype=jnp.float32) / n_freq)
    ang_row = row[:, None] * freqs[None, :]
    ang_col = col[:, None] * freqs[None, :]

    h = x
    for i in range(DEPTH):
        xn = rms_norm_2(h, pre_mix_norm[i])
        proj = xn @ w_in[i]
        o0 = A_WIDTH
        o1 = o0 + A_KV_WIDTH
        o2 = o1 + A_KV_WIDTH
        o3 = o2 + B_WIDTH
        o4 = o3 + B_WIDTH
        qa = proj[..., :o0].reshape(b, s_len, A_KV_HEADS, A_GROUP, HEAD_DIM)
        ka = proj[..., o0:o1].reshape(b, s_len, A_KV_HEADS, HEAD_DIM)
        va = proj[..., o1:o2].reshape(b, s_len, A_KV_HEADS, HEAD_DIM)
        qb = proj[..., o2:o3].reshape(b, s_len, B_HEADS, HEAD_DIM)
        kb = proj[..., o3:o4].reshape(b, s_len, B_HEADS, HEAD_DIM)
        vb = proj[..., o4:].reshape(b, s_len, B_HEADS, HEAD_DIM)

        qa = axial_rope(rms_norm_2(qa, q_norm[i]), ang_row, ang_col)
        ka = axial_rope(rms_norm_2(ka, k_norm[i]), ang_row, ang_col)
        out_a = global_gqa(qa, ka, va).reshape(b, s_len, A_WIDTH)
        out_b = neighbourhood_attn(qb, kb, vb, rel_pos_bias[i], rows).reshape(b, s_len, B_WIDTH)

        mix = jnp.concatenate([out_a, out_b], axis=-1) @ w_o[i]
        h = h + rms_norm_2(mix, post_mix_norm[i])

        m = rms_norm_2(h, pre_mlp_norm[i]) @ w_up[i]
        m = jnp.square(jax.nn.relu(m)) @ w_down[i]
        h = h + rms_norm_2(m, post_mlp_norm[i])

        gate = jax.nn.sigmoid(rms_norm_2(h, pre_ple_norm[i]) @ w_ple_gate[i])
        e = (p[i] @ w_ple_proj[i]) * gate
        h = h + rms_norm_2(e, post_ple_norm[i])
    return h


def setup_inputs(seed=0):
    out = dict(first_inputs(seed))
    for name, value in second_inputs(seed + 1).items():
        if name != "x":
            out[name + "_2"] = value
    return out


def reference(
    x, g_mix, w_in, b_forget, conv_w, conv_b, w_rg, b_rg, w_ig, b_ig, lru_lambda, w_pool,
    pool_scale, w_branch_rnn, w_branch_attn, w_branch_pool, w_out, g_ffn, w_ffn_in, w_ffn_out,
    g_final, p_2, pre_mix_norm_2, w_in_2, q_norm_2, k_norm_2, rel_pos_bias_2, w_o_2,
    post_mix_norm_2, pre_mlp_norm_2, w_up_2, w_down_2, post_mlp_norm_2, pre_ple_norm_2,
    w_ple_gate_2, w_ple_proj_2, post_ple_norm_2,
):
    x = first_block(
        x, g_mix, w_in, b_forget, conv_w, conv_b, w_rg, b_rg, w_ig, b_ig, lru_lambda, w_pool,
        pool_scale, w_branch_rnn, w_branch_attn, w_branch_pool, w_out, g_ffn, w_ffn_in,
        w_ffn_out, g_final,
    )
    return second_block(
        x, p_2, pre_mix_norm_2, w_in_2, q_norm_2, k_norm_2, rel_pos_bias_2, w_o_2,
        post_mix_norm_2, pre_mlp_norm_2, w_up_2, w_down_2, post_mlp_norm_2, pre_ple_norm_2,
        w_ple_gate_2, w_ple_proj_2, post_ple_norm_2,
    )


_drawn_inputs = setup_inputs


def setup_inputs(seed=0):
    import zlib

    import numpy as np

    out = dict(_drawn_inputs(seed))
    spreads = {}
    factors = {'b_rg': 8.0,
     'b_ig': 8.0,
     'q_norm_2': 4.469,
     'k_norm_2': 3.49,
     'pre_ple_norm_2': 5.735,
     'rel_pos_bias_2': 3.885}
    for name, (base, spread) in spreads.items():
        noise = np.random.default_rng([zlib.crc32(name.encode()), seed]).standard_normal(out[name].shape)
        drawn = base * np.exp(spread * noise) if base else spread * noise
        out[name] = __import__('jax').numpy.asarray(drawn.astype(out[name].dtype))
    for name, factor in factors.items():
        out[name] = (out[name] * factor).astype(out[name].dtype)
    return out
```

```python
import math
from contextlib import ExitStack

import concourse.bass as bass
from concourse import mybir

F32 = mybir.dt.float32
F32R = mybir.dt.float32r
ALU = mybir.AluOpType
ACT = mybir.ActivationFunctionType
AX = mybir.AxisListType
ds = bass.ds

P = 128
T = 256
D = 2048
KD = D // P
D_RNN = 1024
HEADS = 8
D_FF = 5632
KF = D_FF // P
D_FF2 = 8192
EPS = 1e-6
SCALE = 128 ** -0.5
RING = 4
BLOCKS = 8
PIECE = BLOCKS * P

STAGE_LIST = [
    ("rnn", 8 * 8, 8 * 4, 8 * 4),
    ("forget", 2, 1, 1),
    ("rnn_branch", 16, 16, 0),
    ("attn", 8 * 12, 8 * 6, 8 * 6),
    ("attn_branch", 16, 16, 0),
    ("pool", 16 * 2, 16, 16),
    ("pool_branch", 16, 16, 0),
    ("out", 32, 16, 0),
    ("up", 2 * 2 * KF, 2 * KF, 2 * KF),
    ("down", 2 * KF, 16, 0),
    ("mix", 2 * 36, 36, 36),
    ("wo", 32, 16, 0),
    ("mlp", 2 * (64 + 64), 2 * (32 + 16), 2 * 32),
    ("ple", 4, 16, 0),
    ("ple_gate", 32, 16, 16),
]


class Stage:

    def __init__(self, piece, tile, scaled):
        self.piece, self.tile, self.scaled = piece, tile, scaled


def plan():
    stages, piece, tile, scaled = {}, 0, 0, 0
    for name, pieces, tiles, normed in STAGE_LIST:
        stages[name] = Stage(piece, tile, scaled)
        piece, tile, scaled = piece + pieces, tile + tiles, scaled + normed
    return stages, piece


STAGES, PIECES = plan()

COLUMN_LIST = [
    ("g_mix", 16), ("g_ffn", 16), ("g_final", 16), ("pre_mix", 16), ("post_mix", 16),
    ("pre_mlp", 16), ("post_mlp", 16), ("pre_ple", 16), ("post_ple", 16),
    ("conv0", 8), ("conv1", 8), ("conv2", 8), ("conv3", 8), ("conv_b", 8),
    ("b_rg", 8), ("b_ig", 8), ("lam", 8), ("pool_scale", 8), ("b_forget", 1), ("q_norm", 1), ("k_norm", 1),
]
COL, NCOL = {}, 0
for _name, _n in COLUMN_LIST:
    COL[_name] = NCOL
    NCOL += _n


class Steps:

    def __init__(self, sem, names):
        self.sem, self.names, self.next = sem, names.split(), 0

    def done(self, name):
        assert self.names[self.next % len(self.names)] == name, (name, self.names, self.next)
        self.next += 1
        return self.sem, 1

    def at(self, name, i=0):
        return i * len(self.names) + self.names.index(name) + 1


def build(nc, w, xT, pT, columns, w_gates, w_pool, rel_bias, near_mask, causal_mask, rope_cos,
          rope_sin, rope_turn, inv_count, unit, outT):
    ctx = ExitStack()
    with ctx:
        def sem(name):
            return ctx.enter_context(nc.semaphore(name))

        SBUF_TOP = nc.sbuf_usable_end
        base = (nc.sbuf_base + 63) // 64 * 64

        def size(shape):
            n = 4
            for s in shape[1:]:
                n *= s
            return -(-n // 64) * 64

        class Area:
            def __init__(self, start, end):
                self.start, self.next, self.end = start, start, end

            def put(self, name, shape, dt=F32):
                t = nc.alloc_sbuf_tensor_at(name, shape, dt, offset=self.next)
                self.next += size(shape)
                assert self.next <= self.end, (name, self.next, self.end)
                return t

        whole = Area(base, SBUF_TOP)
        raw = whole.put("w_raw", [P, RING, PIECE])
        w_hi = whole.put("w_hi", [P, RING, PIECE], F32R)
        w_lo = whole.put("w_lo", [P, RING, PIECE], F32R)
        x = whole.put("x", [P, KD, T])
        h_at = whole.next
        h = whole.put("h", [P, KD, 2 * T], F32R)
        region = whole.next
        REGION = KF * 2 * T * 4
        whole.next += REGION
        low = whole.put("low", [P, 2, T])
        tsum = whole.put("tsum", [P, 2, T])
        tmp = whole.put("tmp", [P, 2, T])
        sq2 = whole.put("sq2", [P, 2, T])
        sqg2 = whole.put("sqg2", [P, 2, T])
        rstd = whole.put("rstd", [P, T])
        rstd_x = whole.put("rstd_x", [P, T])
        root = whole.put("root", [P, T])
        total = whole.put("total", [P, T])
        total_g = whole.put("total_g", [P, T])
        cols = whole.put("cols", [P, NCOL])
        g_both = whole.put("g_both", [P, KD])
        eps = whole.put("eps", [P, 1])
        decay = whole.put("decay", [P, 8])
        ones = whole.put("ones", [P, P])
        ident = whole.put("ident", [P, P])

        def col(name, i=0):
            return cols[:, ds(i + COL[name], 1)]

        a1 = Area(region, region + REGION)
        gate = a1.put("gate", [P, KD, T])
        merged = a1.put("merged", [P, KD, T])
        y = a1.put("y", [P, 8, 2 * T], F32R)
        PADT = 16 + T
        pool_x = a1.put("pool_x", [P, 8, PADT])
        mixers1 = a1.next
        merged_hl = Area(region + 48 * 1024, region + REGION).put("merged_hl", [P, KD, 2 * T], F32R)
        a_rnn = Area(mixers1, region + REGION)
        wgate = a_rnn.put("wgate", [P, 2 * P])
        rx = a_rnn.put("rx", [P, 4 + T])
        u = a_rnn.put("u", [P, T])
        ry = a_rnn.put("ry", [P, T])
        r_g = a_rnn.put("r_g", [P, T])
        i_g = a_rnn.put("i_g", [P, T])
        a_t = a_rnn.put("a_t", [P, T])
        th = a_rnn.put("th", [P, T])
        a2 = a_rnn.put("a2", [P, T])
        gap = a_rnn.put("gap", [P, T])
        sq = a_rnn.put("sq", [P, T])
        iu = a_rnn.put("iu", [P, T])
        b_in = a_rnn.put("b_in", [P, T])
        hid = a_rnn.put("hid", [P, T])
        y2 = a_rnn.put("y2", [P, T])
        y3 = a_rnn.put("y3", [P, T])
        inner = a_rnn.put("inner", [P, T])
        sg = a_rnn.put("sg", [P, T])
        gl = a_rnn.put("gl", [P, T])
        y_r = a_rnn.put("y_r", [P, T])
        ls = a_rnn.put("ls", [P, 8, 8])
        a_att = Area(mixers1, region + REGION)
        fl = a_att.put("fl", [P, T])
        fcum = a_att.put("fcum", [P, T])
        f_t = a_att.put("f_t", [P, 2, P])
        fsel = a_att.put("fsel", [P, T])
        cmask = a_att.put("cmask", [P, 2, T])
        fl_at = a_att.next
        qT = a_att.put("qT", [P, T])
        kT = a_att.put("kT", [P, T])
        vT = a_att.put("vT", [P, T])
        bias = a_att.put("bias", [P, 2, T])
        biasm = a_att.put("biasm", [P, 2, T])
        sc = a_att.put("sc", [P, 2, T])
        pr = a_att.put("pr", [P, 2, T])
        prT = a_att.put("prT", [P, 2, T])
        vtok = a_att.put("vtok", [P, 2, P])
        st = a_att.put("st", [P, 8])
        lf = Area(fl_at, region + REGION).put("lf", [P, 8, T])
        a_pool = Area(mixers1, region + REGION)
        sums = a_pool.put("sums", [P, 2, 2, PADT])
        pooled = a_pool.put("pooled", [P, 8, T])
        inv = a_pool.put("inv", [P, 4, T])
        wpool = a_pool.put("wpool", [P, 4, 2, 2 * P])
        hidden = Area(region, region + REGION).put("hidden", [P, KF, 2 * T], F32R)

        a2_ = Area(region, region + REGION)
        mixed = a2_.put("mixed", [P, 16, 2 * T], F32R)
        mix32 = a2_.put("mix32", [P, KD, T])
        cos_t = a2_.put("cos_t", [P, T])
        sin_t = a2_.put("sin_t", [P, T])
        nmask = a2_.put("nmask", [P, 2, T])
        turn = a2_.put("turn", [P, P])
        rbias = a2_.put("rbias", [P, 2, T])
        rbm = a2_.put("rbm", [P, 2, T])
        rv = a2_.put("rv", [P, T])
        rrs = a2_.put("rrs", [P, T])
        rsq = a2_.put("rsq", [P, T])
        rg = a2_.put("rg", [P, T])
        rcos = a2_.put("rcos", [P, T])
        rsin = a2_.put("rsin", [P, T])
        rsum = a2_.put("rsum", [P, T])
        q_r = a2_.put("q_r", [P, T])
        k_r = a2_.put("k_r", [P, T])
        va = a2_.put("va", [P, T])
        va_tok = a2_.put("va_tok", [P, 2, P])
        qb = a2_.put("qb", [P, T])
        kb = a2_.put("kb", [P, T])
        vb = a2_.put("vb", [P, T])
        vb_tok = a2_.put("vb_tok", [P, 2, P])
        sB = a2_.put("sB", [P, 2, T])
        pA = a2_.put("pA", [P, 2, T])
        pAT = a2_.put("pAT", [P, 2, T])
        pB = a2_.put("pB", [P, 2, T])
        pBT = a2_.put("pBT", [P, 2, T])
        stA = a2_.put("stA", [P, 8])
        stB = a2_.put("stB", [P, 8])
        a3 = Area(region, region + REGION)
        hidden2 = a3.put("hidden2", [P, 32, 2 * T], F32R)
        acc = a3.put("acc", [P, KD, T])
        p_raw = a3.put("p_raw", [P, 2, T])
        p_hl = a3.put("p_hl", [P, 2, 2 * T], F32R)
        e = Area(region, region + REGION).put("e", [P, KD, T])

        ps = [ctx.enter_context(nc.psum_tensor(f"ps_tile{b}", [P, 2 * T], F32)) for b in range(2)]
        psN = ctx.enter_context(nc.psum_tensor("psN", [P, 2 * T], F32))
        psS = ctx.enter_context(nc.psum_tensor("psS", [P, 2, T], F32))
        psF = ctx.enter_context(nc.psum_tensor("psF", [P, 2, T], F32))
        psT = ctx.enter_context(nc.psum_tensor("psT", [P, 2, T], F32))
        psV = ctx.enter_context(nc.psum_tensor("psV", [P, 2 * T], F32))
        psO = ctx.enter_context(nc.psum_tensor("psO", [P, 2 * T], F32))

        landed = [sem(f"piece_landed{r}") for r in range(RING)]
        hi_ready = sem("hi_ready")
        split_done = sem("split_done")
        piece_used = sem("piece_used")
        low_copied = sem("low_copied")
        tile_summed = sem("tile_summed")
        ple_tile_done = sem("ple_tile_done")
        tile_scaled = sem("tile_scaled")
        g_both_ready = sem("g_both_ready")
        squared_mix = sem("squared_mix")
        scaled_mix = sem("scaled_mix")
        post_scaled = sem("post_scaled")
        mix_gained = sem("mix_gained")
        e_gained = sem("e_gained")
        const_landed = sem("const_landed")
        vector_chain = sem("vector_chain")
        scalar_chain = sem("scalar_chain")
        pool_ready = sem("pool_ready")

        def S(names, label):
            return Steps(sem(label), names)

        def tile_matmuls(pe, stage, dp, dt, tile, first_block, chunks, rhs, norm=None, tile_sem=None):
            st_ = STAGES[stage]
            bank = ps[(st_.tile + tile) % 2]
            pe.wait_ge(tile_summed, dt + (st_.tile + tile + 1))
            for c in range(chunks):
                q = first_block + c
                if q % BLOCKS == 0 or c == 0:
                    pe.wait_ge(split_done, dp + (st_.piece + q // BLOCKS + 1))
                slot, b = (st_.piece + q // BLOCKS) % RING, q % BLOCKS
                hi = w_hi[:, slot, b * P:(b + 1) * P]
                lo = w_lo[:, slot, b * P:(b + 1) * P]
                if norm is not None:
                    pe.wait_ge(norm.ready, c + 1)
                a = rhs(c)

                def high():
                    return nc.tensor.matmul(bank[:, :], hi, a, start=c == 0, stop=c == chunks - 1,
                                            skip_group_check=True)

                def cross():
                    return nc.tensor.matmul(bank[:, T:2 * T], lo, a[:, 0:T], start=False, stop=False,
                                            skip_group_check=True)
                if c == 0:
                    high()
                    last = cross()
                else:
                    cross()
                    last = high()
                if q % BLOCKS == BLOCKS - 1:
                    last.then_inc(piece_used, 1)
                elif c == chunks - 1 and tile_sem is not None:
                    last.then_inc(tile_sem, 1)

        def scalar_split(act, stage, dp, k, ahead=RING):
            n = STAGES[stage].piece + k
            if ahead:
                act.wait_ge(piece_used, dp + (n + 1))
            m = n + ahead
            act.wait_ge(landed[m % RING], dp * (16 // RING) + 16 * (m // RING + 1))
            nc.scalar.activation(w_hi[:, m % RING, :], raw[:, m % RING, :], ACT.Copy).then_inc(hi_ready, 1)

        def vector_split(dve, stage, dp, k, ahead=RING):
            m = STAGES[stage].piece + k + ahead
            dve.wait_ge(hi_ready, dp + (m + 1))
            s = m % RING
            nc.vector.tensor_tensor(w_lo[:, s, :], raw[:, s, :], w_hi[:, s, :].bitcast(F32),
                                    ALU.subtract).then_inc(split_done, 1)

        def scalar_low(act, stage, dp, k, tile):
            act.wait_ge(piece_used, dp + (STAGES[stage].piece + k + 1))
            b = (STAGES[stage].tile + tile) % 2
            nc.scalar.activation(low[:, b, :], ps[b][:, T:2 * T], ACT.Copy).then_inc(low_copied, 1)

        def vector_sum(dve, stage, dt, tile, dst):
            n = STAGES[stage].tile + tile
            dve.wait_ge(low_copied, dt + (n + 1))
            nc.vector.tensor_tensor(dst, low[:, n % 2, :], ps[n % 2][:, 0:T], ALU.add)\
                .then_inc(tile_summed, 1)

        def summed(stage, dt, tile):
            return dt + (STAGES[stage].tile + tile + 3)

        class Norm:

            def __init__(self, name):
                self.squared = sem(f"{name}_squared")
                self.added = sem(f"{name}_added")
                self.sums = sem(f"{name}_sums")
                self.root = sem(f"{name}_root")
                self.rstd = sem(f"{name}_rstd")
                self.high = sem(f"{name}_high")
                self.ready = sem(f"{name}_ready")

        norms = {name: Norm(name) for name in ("mix1", "ffn1", "final", "mix2", "mixed2", "mlp2", "mlped2", "ple2",
                                               "pled2")}

        def square_free(act, n, i, b):
            act.wait_ge(n.added, i * 2 + (b + 1))

        def square(act, n, b, src, scale=1.0, buf=None):
            buf = sq2 if buf is None else buf
            nc.scalar.activation(buf[:, b, :], src, ACT.Square, scale=scale).then_inc(n.squared, 1)

        def add_squares(pool, n, chunks=KD, buf=None, into=None):
            buf = sq2 if buf is None else buf
            into = total if into is None else into
            nc.gpsimd.memset(into[:, :], 0.0).then_inc(n.added, 2)
            pool.wait_ge(n.added, 2)
            with nc.gpsimd.Fori(0, chunks // 2) as i:
                for b in range(2):
                    pool.wait_ge(n.squared, i * 2 + (b + 1))
                    pool.wait_ge(n.added, i * 2 + (b + 2))
                    nc.gpsimd.tensor_tensor(into[:, :], into[:, :], buf[:, b, :], ALU.add).then_inc(n.added, 1)

        def norm_tensor(pe, n, src=None, half=0):
            src = total if src is None else src
            pe.wait_ge(n.added, KD + 2)
            nc.tensor.matmul(psN[:, half * T:(half + 1) * T], ones[:, :], src[:, :], start=True, stop=True)\
                .then_inc(n.sums, 1)

        def norm_root(act, n):
            act.wait_ge(n.sums, 1)
            nc.scalar.activation(root[:, :], psN[:, 0:T], ACT.Sqrt, bias=eps[:, 0:1], scale=1.0 / D)\
                .then_inc(n.root, 1)

        def norm_rstd(dve, n, dst=None):
            dve.wait_ge(n.root, 1)
            nc.vector.reciprocal((rstd if dst is None else dst)[:, :], root[:, :]).then_inc(n.rstd, 1)

        def h_high(act, n, c, g):
            nc.scalar.activation(h[:, c, 0:T], x[:, c, :], ACT.Copy, scale=g).then_inc(n.high, 1)

        def h_low(dve, n, i, b, g):
            c = i * 2 + b
            dve.wait_ge(n.high, i * 2 + (b + 1))
            nc.vector.scalar_tensor_tensor(out=h[:, c, T:2 * T], in0=x[:, c, :], scalar=g,
                                           in1=h[:, c, 0:T].bitcast(F32), op0=ALU.mult, op1=ALU.subtract)\
                .then_inc(n.ready, 1)

        def vector_scale(dve, stage, dt, ds_, tile, dst, src):
            dve.wait_ge(tile_summed, summed(stage, dt, tile))
            nc.vector.tensor_tensor(dst, src, rstd[:, :], ALU.mult).then_inc(tile_scaled, 1)

        def scaled(stage, ds_, tile):
            return ds_ + (STAGES[stage].scaled + tile + 1)

        def h_chunk(c):
            return h[:, c, :]

        def merged_chunk(c):
            return merged_hl[:, c, :]

        def y_chunk(c):
            return y[:, c, :]

        rnn_v = S("conv0 conv1 conv2 u inner gap hid y low", "rnn_vector")
        rnn_a = S("r i gelu_sig a th sqrt high", "rnn_scalar")
        rnn_p = S("gates", "rnn_tensor")
        rnn_g = S("y2 y3 iu gl a2 b_in", "rnn_gpsimd")
        wgate_landed = sem("wgate_landed")
        decay_ready = sem("decay_ready")
        branch_mul = {s: sem(f"{s}_gated") for s in ("rnn_branch", "attn_branch", "pool_branch")}
        gates_done = {s: sem(f"{s}_gate_sigmoid") for s in ("rnn", "attn", "pool")}
        forget_p = S("FT", "forget_tensor")
        att_v = S("fsel s max nmax recip p0 p1 vtok low", "attn_vector")
        att_a = S("bias0 bias1 e0 e1 prT high", "attn_scalar")
        att_p = S("scores fk vT pT out", "attn_tensor")
        att_g = S("biasm", "attn_gpsimd")
        pooled_done = sem("pooled_done")
        poolx_pad = sem("poolx_pad")
        pool_p = S("y0 y1 y2 y3", "pool_tensor")
        pool_a = S(" ".join(f"s{c} h{c}" for c in range(8)), "pool_scalar")
        pool_v = S(" ".join(f"l{c}" for c in range(8)), "pool_vector")
        merged_a = S("high0 high1", "merged_high")
        merged_v = S("low0 low1", "merged_low")
        const2_landed = sem("const2_landed")
        const3_landed = sem("const3_landed")
        const4_landed = sem("const4_landed")
        x_added = sem("x_added")
        up_v = S("prod low", "up_vector")
        up_a = S("silu high", "up_scalar")
        down_x = sem("down_x_added")

        kv_v = S("g rstd cos sin sum k vtok", "kv_vector")
        kv_a = S("square root", "kv_scalar")
        kv_p = S("stat turn v", "kv_tensor")
        b2_v = S("g rstd cos sin sum q maxA nmaxA recipA p0A p1A sB maxB nmaxB recipB p0B p1B vtokB lowA lowB",
                 "heads_vector")
        b2_a = S("square root e0A e1A e0B e1B pAT pBT highA highB", "heads_scalar")
        b2_p = S("stat turn scoresA scoresB pTA pTB vTB outA outB", "heads_tensor")
        b2_g = S("rbm", "heads_gpsimd")
        rbias_landed = sem("rbias_landed")
        sq_v = S("sq low", "mlp_vector")
        sq_a = S("high", "mlp_scalar")
        acc_zero = sem("acc_zeroed")
        acc_added = sem("acc_added")
        p_split = sem("p_split")
        ple_a = sem("ple_sigmoid")
        ple_v = sem("ple_gated")
        stored = sem("stored")
        x_landed = [sem(f"x_landed{n}") for n in range(4)]
        x_mixed = sem("x_mixed")
        x_mlped = sem("x_mlped")
        x_final = sem("x_final")
        post_gained = sem("post_gained")
        result_t = sem("result_scaled")
        result_v = sem("result_by_vector")
        result_g = sem("result_by_gpsimd")
        p_landed = sem("p_landed")

        block = ctx.enter_context(nc.Block())

        @block.sync
        def _(sp):
            def load(n, group):
                sp.dma_start(raw[:, n % RING, :], w[group, n % RING]).then_inc(landed[n % RING], 16)

            for n in range(RING):
                c = slice(4 * n, 4 * n + 4)
                sp.dma_start(x[:, c, :], xT[:, c, :]).then_inc(x_landed[n], 16)
                load(n, 0)
            with nc.sync.Fori(1, PIECES // RING) as g:
                for r in range(RING):
                    sp.wait_ge(split_done, g * RING + (r + 1 - RING))
                    load(r, g)
            for r in range(PIECES % RING):
                n = PIECES // RING * RING + r
                sp.wait_ge(split_done, n + 1 - RING)
                load(r, PIECES // RING)
            for quarter in range(4):
                c = slice(4 * quarter, 4 * quarter + 4)
                sp.wait_ge(result_v, min(4 * quarter + 4, RESULT_V))
                if 4 * quarter + 4 > RESULT_V:
                    sp.wait_ge(result_g, 2 * (4 * quarter + 4 - RESULT_V))
                sp.dma_start(outT[:, c, :], x[:, c, :]).then_inc(stored, 16)
            sp.wait_ge(stored, 64)

        @block.gpsimd
        def _(pool):

            def mul(dst, a, b, after, done):
                for s_, v in after:
                    pool.wait_ge(s_, v)
                nc.gpsimd.tensor_tensor(dst, a, b, ALU.mult).then_inc(*done)

            add_squares(pool, norms["mix1"])
            with nc.gpsimd.Fori(0, 8) as i:
                mul(y2[:, :], ry[:, :], ry[:, :], [(tile_scaled, scaled("rnn", i * 4, 1))], rnn_g.done("y2"))
                mul(y3[:, :], y2[:, :], ry[:, :], [(rnn_g.sem, rnn_g.at("y2", i))], rnn_g.done("y3"))
                mul(iu[:, :], i_g[:, :], u[:, :], [(rnn_a.sem, rnn_a.at("i", i))], rnn_g.done("iu"))
                mul(gl[:, :], ry[:, :], sg[:, :], [(rnn_a.sem, rnn_a.at("gelu_sig", i))], rnn_g.done("gl"))
                mul(a2[:, :], a_t[:, :], a_t[:, :], [(rnn_a.sem, rnn_a.at("a", i))], rnn_g.done("a2"))
                mul(b_in[:, :], sq[:, :], iu[:, :], [(rnn_a.sem, rnn_a.at("sqrt", i)), (rnn_g.sem, rnn_g.at("iu", i))],
                    rnn_g.done("b_in"))
            pool.wait_ge(rnn_v.sem, rnn_v.at("low", 7))
            pool.dma_start(cmask[:, :, :], causal_mask).then_inc(const2_landed, 16)
            pool.wait_ge(const2_landed, 16)
            with nc.gpsimd.Fori(0, 8) as i:
                pool.wait_ge(att_a.sem, att_a.at("bias1", i))
                nc.gpsimd.tensor_tensor(biasm[:, :, :], bias[:, :, :], cmask[:, :, :], ALU.add)\
                    .then_inc(*att_g.done("biasm"))
            pool.wait_ge(att_v.sem, att_v.at("low", 7))
            pool.dma_start(inv[:, :, :], inv_count).then_inc(const3_landed, 16)
            pool.dma_start(wpool[:, :, :, :], w_pool).then_inc(const3_landed, 16)
            pool_steps = [0]

            def step(ins):
                pool_steps[0] += 1
                ins.then_inc(pooled_done, 1)
                pool.wait_ge(pooled_done, pool_steps[0])

            step(nc.gpsimd.memset(sums[:, :, :, :], 0.0))
            pool.wait_ge(poolx_pad, 1)
            pool.wait_ge(const3_landed, 32)
            for g in range(4):
                src = pool_x[:, 2 * g:2 * g + 2, :]
                for level in range(g + 1):
                    lag = 1 << level
                    dst = sums[:, level % 2, :, :]
                    step(nc.gpsimd.tensor_tensor(dst[:, :, 16:PADT], src[:, :, 16:PADT],
                                                 src[:, :, 16 - lag:PADT - lag], ALU.add))
                    src = dst
                means = sums[:, (g + 1) % 2, :, 16:PADT]
                for m in range(2):
                    step(nc.gpsimd.tensor_tensor(means[:, m, :], src[:, m, 16:PADT], inv[:, g, :], ALU.mult))
                step(nc.gpsimd.tensor_tensor(pooled[:, 2 * g:2 * g + 2, :], means,
                                             pool_x[:, 2 * g:2 * g + 2, 16:PADT], ALU.subtract))
            pool.wait_ge(norms["mix1"].sums, 1)
            add_squares(pool, norms["ffn1"])
            pool.wait_ge(norms["ffn1"].sums, 1)
            a, b_ = norms["final"], norms["mix2"]
            nc.gpsimd.memset(total[:, :], 0.0).then_inc(a.added, 2)
            nc.gpsimd.memset(total_g[:, :], 0.0).then_inc(b_.added, 2)
            with nc.gpsimd.Fori(0, 8) as i:
                for b in range(2):
                    for n, buf, into in ((a, sq2, total), (b_, sqg2, total_g)):
                        pool.wait_ge(n.squared, i * 2 + (b + 1))
                        pool.wait_ge(n.added, i * 2 + (b + 2))
                        nc.gpsimd.tensor_tensor(into[:, :], into[:, :], buf[:, b, :], ALU.add).then_inc(n.added, 1)
            pool.wait_ge(down_x, 16)
            for dst, src in ((cos_t[:, :], rope_cos), (sin_t[:, :], rope_sin), (turn[:, :], rope_turn),
                             (nmask[:, :, :], near_mask)):
                pool.dma_start(dst, src).then_inc(const4_landed, 16)
            pool.wait_ge(const4_landed, 64)
            with nc.gpsimd.Fori(0, 8) as i:
                pool.wait_ge(rbias_landed, i * 16 + 16)
                nc.gpsimd.tensor_tensor(rbm[:, :, :], rbias[:, :, :], nmask[:, :, :], ALU.add)\
                    .then_inc(*b2_g.done("rbm"))
            pool.wait_ge(b2_v.sem, b2_v.at("lowB", 7))
            pool.dma_start(p_raw[:, :, :], pT).then_inc(p_landed, 16)

            def update(n, src):
                pool.wait_ge(n.rstd, 1)
                for c in range(KD):
                    nc.gpsimd.tensor_tensor(src[:, c, :], src[:, c, :], rstd_x[:, :], ALU.mult)\
                        .then_inc(post_scaled, 1)

            pool.wait_ge(norms["mix2"].sums, 1)
            add_squares(pool, norms["mixed2"])
            update(norms["mixed2"], mix32)
            add_squares(pool, norms["mlp2"])
            pool.wait_ge(norms["mlp2"].sums, 1)
            add_squares(pool, norms["mlped2"])
            update(norms["mlped2"], acc)
            add_squares(pool, norms["ple2"])
            pool.wait_ge(norms["ple2"].sums, 1)
            add_squares(pool, norms["pled2"])
            pool.wait_ge(norms["pled2"].rstd, 1)
            for k, c in enumerate(range(RESULT_V, KD)):
                nc.gpsimd.tensor_tensor(e[:, c, :], e[:, c, :], rstd_x[:, :], ALU.mult).then_inc(result_g, 1)
                pool.wait_ge(result_g, 2 * k + 1)
                nc.gpsimd.tensor_tensor(x[:, c, :], x[:, c, :], e[:, c, :], ALU.add).then_inc(result_g, 1)

        POOL_STEPS = 1 + sum(g + 1 + 3 for g in range(4))
        POOLED = [1 + sum(k + 1 + 3 for k in range(g + 1)) for g in range(4)]

        @block.scalar
        def _(act):
            def split(stage, dp, k):
                scalar_split(act, stage, dp, k)

            def act_op(dst, src, fn, after, done, **kw):
                for s_, v in after:
                    act.wait_ge(s_, v)
                return nc.scalar.activation(dst, src, fn, **kw).then_inc(*done)

            act.dma_start(cols[:, :], columns).then_inc(const_landed, 16)
            act.dma_start(ident[:, :], unit).then_inc(const_landed, 16)
            for k in range(RING):
                act.wait_ge(x_landed[k], 16)
                if k == 0:
                    act.wait_ge(const_landed, 32)
                for c in range(4 * k, 4 * k + 4):
                    h_high(act, norms["mix1"], c, col("g_mix", c))
                scalar_split(act, "rnn", 0, k, ahead=0)
                for c in range(4 * k, 4 * k + 4):
                    square_free(act, norms["mix1"], c // 2, c % 2)
                    square(act, norms["mix1"], c % 2, x[:, c, :])
            act.wait_ge(vector_chain, 3)
            norm_root(act, norms["mix1"])
            act_op(ls[:, 3, :], ls[:, 2, :], ACT.Exp, [(vector_chain, 6)], (scalar_chain, 1), scale=-1.0)

            act.wait_ge(decay_ready, 1)
            with nc.scalar.Fori(0, 8) as i:
                dp, dt = i * 8, i * 4
                act.dma_start(wgate[:, :], w_gates[i]).then_inc(wgate_landed, 16)
                split("rnn", dp, 0)
                scalar_low(act, "rnn", dp, 1, 0)
                split("rnn", dp, 1)
                split("rnn", dp, 2)
                scalar_low(act, "rnn", dp, 3, 1)
                split("rnn", dp, 3)
                split("rnn", dp, 4)
                act_op(r_g[:, :], psS[:, 0, :], ACT.Sigmoid, [(rnn_p.sem, rnn_p.at("gates", i))],
                       rnn_a.done("r"), bias=col("b_rg", i))
                act_op(i_g[:, :], psS[:, 1, :], ACT.Sigmoid, [], rnn_a.done("i"), bias=col("b_ig", i))
                act_op(sg[:, :], inner[:, :], ACT.Sigmoid, [(rnn_v.sem, rnn_v.at("inner", i))],
                       rnn_a.done("gelu_sig"), scale=2.0 * math.sqrt(2.0 / math.pi))
                act_op(a_t[:, :], r_g[:, :], ACT.Exp, [(rnn_a.sem, rnn_a.at("r", i))], rnn_a.done("a"),
                       scale=decay[:, ds(i, 1)])
                act_op(th[:, :], r_g[:, :], ACT.Tanh, [], rnn_a.done("th"), scale=decay[:, ds(i, 1)])
                scalar_low(act, "rnn", dp, 5, 2)
                split("rnn", dp, 5)
                split("rnn", dp, 6)
                act_op(sq[:, :], gap[:, :], ACT.Sqrt, [(rnn_v.sem, rnn_v.at("gap", i))], rnn_a.done("sqrt"),
                       scale=-1.0)
                scalar_low(act, "rnn", dp, 7, 3)
                split("rnn", dp, 7)
                for b in range(2):
                    act_op(gate[:, i * 2 + b, :], tsum[:, b, :], ACT.Sigmoid,
                           [(tile_scaled, scaled("rnn", dt, 2 + b))], (gates_done["rnn"], 1))
                act_op(y[:, i, 0:T], y_r[:, :], ACT.Copy, [(rnn_v.sem, rnn_v.at("y", i))], rnn_a.done("high"))

            split("forget", 0, 0)
            scalar_low(act, "forget", 0, 1, 0)
            split("forget", 0, 1)
            act_op(lf[:, 3, :], lf[:, 2, :], ACT.Exp, [(vector_chain, LS_STEPS + 3)],
                   (scalar_chain, 1), scale=-1.0)

            def branch(stage):
                with nc.scalar.Fori(0, 4) as i:
                    for t in range(4):
                        scalar_low(act, stage, i * 4, t, t)
                        split(stage, i * 4, t)

            branch("rnn_branch")

            with nc.scalar.Fori(0, 8) as i:
                dp, dt = i * 12, i * 6
                for k in range(6):
                    if k % 2:
                        scalar_low(act, "attn", dp, k, k // 2)
                    split("attn", dp, k)
                split("attn", dp, 6)
                for b in range(2):
                    act_op(bias[:, b, :], psF[:, 0, :], ACT.Identity, [(att_p.sem, att_p.at("fk", i))],
                           att_a.done(f"bias{b}"), scale=-1.0, bias=f_t[:, b, ds(i, 1)])
                scalar_low(act, "attn", dp, 7, 3)
                split("attn", dp, 7)
                for b in range(2):
                    act_op(pr[:, b, :], sc[:, b, :], ACT.Exp, [(att_v.sem, att_v.at("nmax", i))],
                           att_a.done(f"e{b}"), bias=st[:, 2 + b:3 + b], accum_out=st[:, 4 + b:5 + b])
                split("attn", dp, 8)
                scalar_low(act, "attn", dp, 9, 4)
                split("attn", dp, 9)
                split("attn", dp, 10)
                act_op(prT[:, :, :], psT[:, :, :], ACT.Copy, [(att_p.sem, att_p.at("pT", i))], att_a.done("prT"))
                scalar_low(act, "attn", dp, 11, 5)
                split("attn", dp, 11)
                for b in range(2):
                    act_op(gate[:, i * 2 + b, :], tsum[:, b, :], ACT.Sigmoid,
                           [(tile_scaled, scaled("attn", dt, 4 + b))], (gates_done["attn"], 1))
                act_op(y[:, i, 0:T], psO[:, 0:T], ACT.Copy, [(att_p.sem, att_p.at("out", i))], att_a.done("high"))
            branch("attn_branch")

            with nc.scalar.Fori(0, 8) as i:
                for b in range(2):
                    split("pool", i * 4, 2 * b)
                    scalar_low(act, "pool", i * 4, 2 * b + 1, b)
                    split("pool", i * 4, 2 * b + 1)
                    act_op(gate[:, i * 2 + b, :], tsum[:, b, :], ACT.Sigmoid,
                           [(tile_scaled, scaled("pool", i * 2, b))], (gates_done["pool"], 1))
            for c in range(8):
                g, m = c // 2, c % 2
                bank = (psS, psF, psT)[g % 3]
                act_op(tmp[:, m, :], bank[:, m, :], ACT.Identity, [(pool_p.sem, pool_p.at(f"y{g}"))]
                       + ([(pool_v.sem, pool_v.at(f"l{c - 2}"))] if c >= 2 else []),
                       pool_a.done(f"s{c}"), scale=col("pool_scale", c))
                act_op(y[:, c, 0:T], tmp[:, m, :], ACT.Copy, [(pool_a.sem, pool_a.at(f"s{c}"))],
                       pool_a.done(f"h{c}"))
            branch("pool_branch")
            for half in range(2):
                c = slice(8 * half, 8 * half + 8)
                act_op(merged_hl[:, c, 0:T], merged[:, c, :], ACT.Copy, [(branch_mul["pool_branch"], 32)],
                       merged_a.done(f"high{half}"))

            def plain(stage, tiles, per_tile, body=2):
                with nc.scalar.Fori(0, tiles // body) as i:
                    for t in range(body):
                        for k in range(per_tile):
                            if k == per_tile - 1:
                                scalar_low(act, stage, i * (body * per_tile), t * per_tile + k, t)
                            split(stage, i * (body * per_tile), t * per_tile + k)

            with nc.scalar.Fori(0, 8) as i:
                for b in range(2):
                    split("out", i * 4, 2 * b)
                    scalar_low(act, "out", i * 4, 2 * b + 1, b)
                    split("out", i * 4, 2 * b + 1)
                    square_free(act, norms["ffn1"], i, b)
                    act.wait_ge(x_added, i * 2 + (b + 1))
                    h_high(act, norms["ffn1"], i * 2 + b, col("g_ffn", i * 2 + b))
                    square(act, norms["ffn1"], b, x[:, i * 2 + b, :])
            norm_root(act, norms["ffn1"])
            with nc.scalar.Fori(0, KF) as i:
                dp, dt = i * 4, i * 2
                split("up", dp, 0)
                scalar_low(act, "up", dp, 1, 0)
                split("up", dp, 1)
                act_op(tmp[:, 1, :], tsum[:, 0, :], ACT.Silu, [(tile_scaled, scaled("up", dt, 0))],
                       up_a.done("silu"))
                split("up", dp, 2)
                scalar_low(act, "up", dp, 3, 1)
                split("up", dp, 3)
                act_op(hidden[:, i, 0:T], tmp[:, 0, :], ACT.Copy, [(up_v.sem, up_v.at("prod", i))],
                       up_a.done("high"))
            with nc.scalar.Fori(0, 2) as i:
                for k in range(KF):
                    for t in DOWN_ENDS.get(k, []):
                        scalar_low(act, "down", i * KF, k, t)
                    split("down", i * KF, k)
                    for t in DOWN_ENDS.get(k, []):
                        c = i * 8 + t
                        square_free(act, norms["final"], i * 4 + t // 2, t % 2)
                        square_free(act, norms["mix2"], i * 4 + t // 2, t % 2)
                        act.wait_ge(down_x, i * 8 + (t + 1))
                        h_high(act, norms["mix2"], c, g_both[:, ds(c, 1)])
                        square(act, norms["final"], t % 2, x[:, c, :])
                        square(act, norms["mix2"], t % 2, x[:, c, :], col("g_final", c), sqg2)
            act.wait_ge(norms["mix2"].sums, 1)
            norm_root(act, norms["final"])
            act.wait_ge(squared_mix, 2)
            nc.scalar.activation(root[:, :], tmp[:, 1, :], ACT.Sqrt, bias=eps[:, 0:1], scale=1.0 / D)\
                .then_inc(norms["mix2"].root, 1)

            act.wait_ge(down_x, 16)
            with nc.scalar.Fori(0, 2) as j:
                dp = j * 36
                split("mix", dp, 0)
                scalar_low(act, "mix", dp, 1, 0)
                split("mix", dp, 1)
                act_op(rsq[:, :], rv[:, :], ACT.Square, [(tile_scaled, scaled("mix", j * 18, 0))],
                       kv_a.done("square"))
                split("mix", dp, 2)
                scalar_low(act, "mix", dp, 3, 1)
                split("mix", dp, 3)
                act_op(root[:, :], psN[:, 0:T], ACT.Sqrt, [(kv_p.sem, kv_p.at("turn", j))], kv_a.done("root"),
                       bias=eps[:, 0:1], scale=1.0 / P)
                with nc.scalar.Fori(0, 4) as i:
                    m = j * 4 + i
                    dp, dt = j * 36 + i * 8, j * 18 + i * 4
                    act.dma_start(rbias[:, :, :], rel_bias[m]).then_inc(rbias_landed, 16)
                    split("mix", dp, 4)
                    scalar_low(act, "mix", dp, 5, 2)
                    split("mix", dp, 5)
                    act_op(rsq[:, :], rv[:, :], ACT.Square, [(tile_scaled, scaled("mix", dt, 2))],
                           b2_a.done("square"))
                    split("mix", dp, 6)
                    scalar_low(act, "mix", dp, 7, 3)
                    split("mix", dp, 7)
                    act_op(root[:, :], psN[:, 0:T], ACT.Sqrt, [(b2_p.sem, b2_p.at("turn", m))],
                           b2_a.done("root"), bias=eps[:, 0:1], scale=1.0 / P)
                    split("mix", dp, 8)
                    scalar_low(act, "mix", dp, 9, 4)
                    split("mix", dp, 9)
                    for b in range(2):
                        act_op(pA[:, b, :], psS[:, b, :], ACT.Exp, [(b2_v.sem, b2_v.at("nmaxA", m))],
                               b2_a.done(f"e{b}A"), scale=SCALE, bias=stA[:, 2 + b:3 + b],
                               accum_out=stA[:, 4 + b:5 + b])
                    for b in range(2):
                        act_op(pB[:, b, :], sB[:, b, :], ACT.Exp, [(b2_v.sem, b2_v.at("nmaxB", m))],
                               b2_a.done(f"e{b}B"), bias=stB[:, 2 + b:3 + b], accum_out=stB[:, 4 + b:5 + b])
                    split("mix", dp, 10)
                    scalar_low(act, "mix", dp, 11, 5)
                    split("mix", dp, 11)
                    act_op(pAT[:, :, :], psT[:, :, :], ACT.Copy, [(b2_p.sem, b2_p.at("pTA", m))],
                           b2_a.done("pAT"))
                    act_op(pBT[:, :, :], psS[:, :, :], ACT.Copy, [(b2_p.sem, b2_p.at("pTB", m))],
                           b2_a.done("pBT"))
                    act_op(mixed[:, m, 0:T], psO[:, 0:T], ACT.Copy, [(b2_p.sem, b2_p.at("outA", m))],
                           b2_a.done("highA"))
                    act_op(mixed[:, m + 8, 0:T], psN[:, 0:T], ACT.Copy, [(b2_p.sem, b2_p.at("outB", m))],
                           b2_a.done("highB"))
            with nc.scalar.Fori(0, 8) as i:
                for b in range(2):
                    split("wo", i * 4, 2 * b)
                    scalar_low(act, "wo", i * 4, 2 * b + 1, b)
                    split("wo", i * 4, 2 * b + 1)
                    square_free(act, norms["mixed2"], i, b)
                    act.wait_ge(tile_summed, summed("wo", i * 2, b))
                    square(act, norms["mixed2"], b, tsum[:, b, :])
                    nc.scalar.activation(mix32[:, i * 2 + b, :], tsum[:, b, :], ACT.Copy,
                                         scale=col("post_mix", i * 2 + b)).then_inc(mix_gained, 1)

            def updated(n, before, added):
                norm_root(act, before)
                with nc.scalar.Fori(0, 8) as i:
                    for b in range(2):
                        square_free(act, n, i, b)
                        act.wait_ge(added, i * 2 + (b + 1))
                        h_high(act, n, i * 2 + b, col("pre_mlp" if n is norms["mlp2"] else "pre_ple", i * 2 + b))
                        square(act, n, b, x[:, i * 2 + b, :])
                norm_root(act, n)

            updated(norms["mlp2"], norms["mixed2"], x_mixed)

            with nc.scalar.Fori(0, 2) as j:
                with nc.scalar.Fori(0, 16) as i:
                    dp = j * 128 + i * 4
                    for b in range(2):
                        split("mlp", dp, 2 * b)
                        scalar_low(act, "mlp", dp, 2 * b + 1, b)
                        split("mlp", dp, 2 * b + 1)
                        act_op(hidden2[:, i * 2 + b, 0:T], tmp[:, b, :], ACT.Copy,
                               [(sq_v.sem, sq_v.at("sq", j * 32 + i * 2 + b))], sq_a.done("high"))
                with nc.scalar.Fori(0, 8) as i:
                    dp = j * 128 + i * 8
                    for k in range(8):
                        if k % 4 == 3:
                            scalar_low(act, "mlp", dp, 64 + k, k // 4)
                        split("mlp", dp, 64 + k)

            act.wait_ge(acc_added, 32)
            act_op(p_hl[:, :, 0:T], p_raw[:, :, :], ACT.Copy, [(p_landed, 16)], (p_split, 1))
            for t in range(16):
                k = t // 4
                if t % 4 < 3:
                    act.wait_ge(ple_tile_done, 3 * k + t % 4 + 1)
                    b = (STAGES["ple"].tile + t) % 2
                    nc.scalar.activation(low[:, b, :], ps[b][:, T:2 * T], ACT.Copy).then_inc(low_copied, 1)
                else:
                    scalar_low(act, "ple", 0, k, t)
                    split("ple", 0, k)
                square_free(act, norms["mlped2"], t // 2, t % 2)
                square(act, norms["mlped2"], t % 2, acc[:, t, :])
                nc.scalar.activation(acc[:, t, :], acc[:, t, :], ACT.Copy, scale=col("post_mlp", t))\
                    .then_inc(post_gained, 1)
            updated(norms["ple2"], norms["mlped2"], x_mlped)

            def embed(i, last):
                for b in range(2):
                    if not last:
                        split("ple_gate", i * 4, 2 * b)
                    scalar_low(act, "ple_gate", i * 4, 2 * b + 1, b)
                    if not last:
                        split("ple_gate", i * 4, 2 * b + 1)
                    act_op(tmp[:, b, :], tsum[:, b, :], ACT.Sigmoid,
                           [(tile_scaled, scaled("ple_gate", i * 2, b))], (ple_a, 1))
                    square_free(act, norms["pled2"], i, b)
                    act.wait_ge(ple_v, i * 2 + (b + 1))
                    c = i * 2 + b
                    square(act, norms["pled2"], b, e[:, c, :])
                    nc.scalar.activation(e[:, c, :], e[:, c, :], ACT.Copy, scale=col("post_ple", c))\
                        .then_inc(e_gained, 1)

            with nc.scalar.Fori(0, 7) as i:
                embed(i, False)
            embed(7, True)
            norm_root(act, norms["pled2"])

        @block.vector
        def _(dve):
            chain = [0]

            def link(ins):
                chain[0] += 1
                ins.then_inc(vector_chain, 1)
                dve.wait_ge(vector_chain, chain[0])

            def split(stage, dp, k):
                vector_split(dve, stage, dp, k)

            def vsum(stage, dt, tile, dst):
                vector_sum(dve, stage, dt, tile, dst)

            def vscaled(stage, dt, tile, sums, dst=None, ds_=None):
                vsum(stage, dt, tile, sums)
                vector_scale(dve, stage, dt, ds_, tile, sums if dst is None else dst, sums)

            def tt(dst, a, b, op, after, done):
                for s_, v in after:
                    dve.wait_ge(s_, v)
                nc.vector.tensor_tensor(dst, a, b, op).then_inc(*done)

            def ts(dst, a, s1, s2, op0, op1, after, done):
                for s_, v in after:
                    dve.wait_ge(s_, v)
                if s2 is None:
                    nc.vector.tensor_scalar(dst, a, s1, None, op0).then_inc(*done)
                else:
                    nc.vector.tensor_scalar(dst, a, s1, s2, op0, op1).then_inc(*done)

            def stt(dst, a, s1, b, op0, op1, after, done):
                for s_, v in after:
                    dve.wait_ge(s_, v)
                nc.vector.scalar_tensor_tensor(out=dst, in0=a, scalar=s1, in1=b, op0=op0, op1=op1).then_inc(*done)

            def log_sigmoid(buf, exp_count, factor):
                B = lambda k: buf[:, k, :]
                link(nc.vector.tensor_scalar(B(1), B(0), -1.0, None, ALU.mult))
                link(nc.vector.tensor_tensor(B(2), B(0), B(1), ALU.max))
                dve.wait_ge(scalar_chain, exp_count)
                link(nc.vector.tensor_scalar(B(4), B(3), 2.0, None, ALU.add))
                link(nc.vector.reciprocal(B(5), B(4)))
                link(nc.vector.tensor_tensor(B(4), B(3), B(5), ALU.mult))
                link(nc.vector.tensor_tensor(B(5), B(4), B(4), ALU.mult))
                link(nc.vector.tensor_scalar(B(6), B(5), 1.0 / 19.0, None, ALU.mult))
                for odd in (17, 15, 13, 11, 9, 7, 5, 3):
                    link(nc.vector.scalar_tensor_tensor(out=B(6), in0=B(6), scalar=1.0 / odd, in1=B(5),
                                                        op0=ALU.add, op1=ALU.mult))
                link(nc.vector.scalar_tensor_tensor(out=B(6), in0=B(6), scalar=1.0, in1=B(4),
                                                    op0=ALU.add, op1=ALU.mult))
                link(nc.vector.tensor_scalar(B(1), B(0), 0.0, factor, ALU.min, ALU.mult))
                link(nc.vector.scalar_tensor_tensor(out=B(7), in0=B(6), scalar=-2.0 * factor, in1=B(1),
                                                    op0=ALU.mult, op1=ALU.add))

            nc.vector.memset(rx[:, :], 0.0).then_inc(tile_summed, 2)
            link(nc.vector.memset(eps[:, :], EPS))
            link(nc.vector.memset(ones[:, :], 1.0))
            link(nc.vector.memset(pool_x[:, :, 0:16], 0.0))
            dve.wait_ge(const_landed, 32)
            for k in range(RING):
                for c in range(4 * k, 4 * k + 4):
                    h_low(dve, norms["mix1"], c // 2, c % 2, col("g_mix", c))
                vector_split(dve, "rnn", 0, k, ahead=0)
            nc.vector.tensor_tensor(g_both[:, :], cols[:, COL["g_final"]:COL["g_final"] + KD],
                                    cols[:, COL["pre_mix"]:COL["pre_mix"] + KD], ALU.mult).then_inc(g_both_ready, 1)
            norm_rstd(dve, norms["mix1"])
            link(nc.vector.tensor_copy(ls[:, 0, :], cols[:, COL["lam"]:COL["lam"] + 8]))
            log_sigmoid(ls, 1, 8.0)
            assert chain[0] == LS_STEPS
            nc.vector.tensor_copy(decay[:, :], ls[:, 7, :]).then_inc(decay_ready, 1)

            with nc.vector.Fori(0, 8) as i:
                dp, dt = i * 8, i * 4
                V = lambda name: (rnn_v.sem, rnn_v.at(name, i))
                split("rnn", dp, 0)
                vscaled("rnn", dt, 0, tsum[:, 0, :], rx[:, 3:3 + T])
                split("rnn", dp, 1)
                ts(u[:, :], rx[:, 0:T], col("conv0", i), col("conv_b", i), ALU.mult, ALU.add,
                   [(tile_scaled, scaled("rnn", dt, 0))], rnn_v.done("conv0"))
                for k, (before, name) in enumerate((("conv0", "conv1"), ("conv1", "conv2"), ("conv2", "u")), 1):
                    stt(u[:, :], rx[:, k:k + T], col(f"conv{k}", i), u[:, :], ALU.mult, ALU.add,
                        [V(before)], rnn_v.done(name))
                split("rnn", dp, 2)
                vscaled("rnn", dt, 1, tsum[:, 1, :], ry[:, :])
                split("rnn", dp, 3)
                split("rnn", dp, 4)
                stt(inner[:, :], y3[:, :], 0.044715, ry[:, :], ALU.mult, ALU.add,
                    [(rnn_g.sem, rnn_g.at("y3", i))], rnn_v.done("inner"))
                vscaled("rnn", dt, 2, tsum[:, 0, :])
                split("rnn", dp, 5)
                stt(gap[:, :], a2[:, :], 1.0, th[:, :], ALU.add, ALU.mult,
                    [(rnn_g.sem, rnn_g.at("a2", i)), (rnn_a.sem, rnn_a.at("th", i))], rnn_v.done("gap"))
                split("rnn", dp, 6)
                vscaled("rnn", dt, 3, tsum[:, 1, :])
                split("rnn", dp, 7)
                dve.wait_ge(rnn_g.sem, rnn_g.at("b_in", i))
                nc.vector.tensor_tensor_scan(hid[:, :], a_t[:, :], b_in[:, :], 0.0, ALU.mult, ALU.add)\
                    .then_inc(*rnn_v.done("hid"))
                tt(y_r[:, :], gl[:, :], hid[:, :], ALU.mult, [V("hid")], rnn_v.done("y"))
                tt(y[:, i, T:2 * T], y_r[:, :], y[:, i, 0:T].bitcast(F32), ALU.subtract,
                   [(rnn_a.sem, rnn_a.at("high", i))], rnn_v.done("low"))

            split("forget", 0, 0)
            vscaled("forget", 0, 0, fl[:, :])
            split("forget", 0, 1)
            dve.wait_ge(tile_scaled, scaled("forget", 0, 0))
            link(nc.vector.tensor_scalar(lf[:, 0, :], fl[:, :], cols[:, COL["b_forget"]:COL["b_forget"] + 1],
                                         None, ALU.add))
            log_sigmoid(lf, 2, 1.0)
            link(nc.vector.memset(lf[:, 0, :], 1.0))
            link(nc.vector.tensor_tensor_scan(fcum[:, :], lf[:, 0, :], lf[:, 7, :], 0.0, ALU.mult, ALU.add))
            assert chain[0] == F_STEPS

            def branch(stage, gates):
                muls = branch_mul[stage]
                first = stage == "rnn_branch"
                per = 1 if first else 2
                dve.wait_ge(gates_done[gates], 16)
                with nc.vector.Fori(0, 4) as i:
                    for t in range(4):
                        vsum(stage, i * 4, t, tsum[:, t % 2, :])
                        split(stage, i * 4, t)
                        o = i * 4 + t
                        dst = merged[:, o, :] if first else tmp[:, t % 2, :]
                        tt(dst, gate[:, o, :], tsum[:, t % 2, :], ALU.mult,
                           [(tile_summed, summed(stage, i * 4, t))], (muls, 1))
                        if not first:
                            tt(merged[:, o, :], merged[:, o, :], tmp[:, t % 2, :], ALU.add,
                               [(muls, i * 8 + (2 * t + 1))], (muls, 1))

            branch("rnn_branch", "rnn")
            dve.wait_ge(forget_p.sem, forget_p.at("FT"))
            link(nc.vector.tensor_copy(f_t[:, :, :], psV[:, 0:2 * P].rearrange("p (b q) -> p b q", b=2)))

            with nc.vector.Fori(0, 8) as i:
                dp, dt = i * 12, i * 6
                V = lambda name: (att_v.sem, att_v.at(name, i))
                split("attn", dp, 0)
                vscaled("attn", dt, 0, qT[:, :])
                split("attn", dp, 1)
                ts(fsel[:, :], fcum[:, :], ident[:, ds(i, 1)], None, ALU.mult, None, [], att_v.done("fsel"))
                split("attn", dp, 2)
                vscaled("attn", dt, 1, kT[:, :])
                split("attn", dp, 3)
                split("attn", dp, 4)
                vscaled("attn", dt, 2, vT[:, :])
                split("attn", dp, 5)
                split("attn", dp, 6)
                stt(sc[:, :, :], psS[:, :, :], SCALE, biasm[:, :, :], ALU.mult, ALU.add,
                    [(att_p.sem, att_p.at("scores", i)), (att_g.sem, att_g.at("biasm", i))], att_v.done("s"))
                dve.wait_ge(*V("s"))
                nc.vector.tensor_reduce(st[:, 0:2], sc[:, :, :], AX.X, ALU.max).then_inc(*att_v.done("max"))
                ts(st[:, 2:4], st[:, 0:2], -1.0, None, ALU.mult, None, [V("max")], att_v.done("nmax"))
                vscaled("attn", dt, 3, tsum[:, 1, :], pool_x[:, i, 16:PADT])
                split("attn", dp, 7)
                dve.wait_ge(att_a.sem, att_a.at("e1", i))
                nc.vector.reciprocal(st[:, 6:8], st[:, 4:6]).then_inc(*att_v.done("recip"))
                for b in range(2):
                    ts(pr[:, b, :], pr[:, b, :], st[:, 6 + b:7 + b], None, ALU.mult, None, [V("recip")],
                       att_v.done(f"p{b}"))
                split("attn", dp, 8)
                dve.wait_ge(att_p.sem, att_p.at("vT", i))
                nc.vector.tensor_copy(vtok[:, :, :], psV[:, 0:2 * P].rearrange("p (b q) -> p b q", b=2))\
                    .then_inc(*att_v.done("vtok"))
                vscaled("attn", dt, 4, tsum[:, 0, :])
                split("attn", dp, 9)
                split("attn", dp, 10)
                vscaled("attn", dt, 5, tsum[:, 1, :])
                split("attn", dp, 11)
                tt(y[:, i, T:2 * T], psO[:, 0:T], y[:, i, 0:T].bitcast(F32), ALU.subtract,
                   [(att_a.sem, att_a.at("high", i))], att_v.done("low"))
            dve.wait_ge(tile_scaled, scaled("attn", 42, 5))
            nc.vector.memset(tmp[:, 1, 0:1], 0.0).then_inc(poolx_pad, 1)
            branch("attn_branch", "attn")

            with nc.vector.Fori(0, 8) as i:
                for b in range(2):
                    split("pool", i * 4, 2 * b)
                    vscaled("pool", i * 2, b, tsum[:, b, :])
                    split("pool", i * 4, 2 * b + 1)
            for c in range(8):
                tt(y[:, c, T:2 * T], tmp[:, c % 2, :], y[:, c, 0:T].bitcast(F32), ALU.subtract,
                   [(pool_a.sem, pool_a.at(f"h{c}"))], pool_v.done(f"l{c}"))
            branch("pool_branch", "pool")
            for half in range(2):
                c = slice(8 * half, 8 * half + 8)
                tt(merged_hl[:, c, T:2 * T], merged[:, c, :], merged_hl[:, c, 0:T].bitcast(F32), ALU.subtract,
                   [(merged_a.sem, merged_a.at(f"high{half}"))], merged_v.done(f"low{half}"))

            with nc.vector.Fori(0, 8) as i:
                for b in range(2):
                    split("out", i * 4, 2 * b)
                    vsum("out", i * 2, b, tsum[:, b, :])
                    tt(x[:, i * 2 + b, :], x[:, i * 2 + b, :], tsum[:, b, :], ALU.add,
                       [(tile_summed, summed("out", i * 2, b))], (x_added, 1))
                    split("out", i * 4, 2 * b + 1)
                    h_low(dve, norms["ffn1"], i, b, col("g_ffn", i * 2 + b))
            norm_rstd(dve, norms["ffn1"])
            with nc.vector.Fori(0, KF) as i:
                dp, dt = i * 4, i * 2
                split("up", dp, 0)
                vscaled("up", dt, 0, tsum[:, 0, :])
                split("up", dp, 1)
                split("up", dp, 2)
                vscaled("up", dt, 1, tsum[:, 1, :])
                tt(tmp[:, 0, :], tmp[:, 1, :], tsum[:, 1, :], ALU.mult,
                   [(up_a.sem, up_a.at("silu", i)), (tile_scaled, scaled("up", dt, 1))], up_v.done("prod"))
                split("up", dp, 3)
                tt(hidden[:, i, T:2 * T], tmp[:, 0, :], hidden[:, i, 0:T].bitcast(F32), ALU.subtract,
                   [(up_a.sem, up_a.at("high", i))], up_v.done("low"))
            with nc.vector.Fori(0, 2) as i:
                for k in range(KF):
                    for t in DOWN_ENDS.get(k, []):
                        vsum("down", i * 8, t, tsum[:, t % 2, :])
                        tt(x[:, i * 8 + t, :], x[:, i * 8 + t, :], tsum[:, t % 2, :], ALU.add,
                           [(tile_summed, summed("down", i * 8, t))], (down_x, 1))
                    split("down", i * KF, k)
                    for t in DOWN_ENDS.get(k, []):
                        h_low(dve, norms["mix2"], i * 4 + t // 2, t % 2, g_both[:, ds(i * 8 + t, 1)])
            norm_rstd(dve, norms["final"], rstd_x)
            dve.wait_ge(norms["final"].rstd, 1)
            tt(tmp[:, 0, :], psN[:, T:2 * T], rstd_x[:, :], ALU.mult, [(norms["mix2"].sums, 1)], (squared_mix, 1))
            tt(tmp[:, 1, :], tmp[:, 0, :], rstd_x[:, :], ALU.mult, [(squared_mix, 1)], (squared_mix, 1))
            norm_rstd(dve, norms["mix2"])
            tt(rstd[:, :], rstd[:, :], rstd_x[:, :], ALU.mult, [(norms["mix2"].rstd, 1)], (scaled_mix, 1))
            dve.wait_ge(scaled_mix, 1)

            dve.wait_ge(const4_landed, 64)

            def rope(steps, scal, tens, g, i, dst, name):
                W = lambda s: (steps.sem, steps.at(s, i))
                dve.wait_ge(scal.sem, scal.at("root", i))
                nc.vector.reciprocal(rrs[:, :], root[:, :]).then_inc(*steps.done("rstd"))
                tt(rcos[:, :], rg[:, :], cos_t[:, :], ALU.mult, [], steps.done("cos"))
                tt(rsin[:, :], psN[:, T:2 * T], sin_t[:, :], ALU.mult, [], steps.done("sin"))
                tt(rsum[:, :], rcos[:, :], rsin[:, :], ALU.add, [W("sin")], steps.done("sum"))
                tt(dst, rsum[:, :], rrs[:, :], ALU.mult, [W("sum")], steps.done(name))

            with nc.vector.Fori(0, 2) as j:
                dp, dt = j * 36, j * 18
                split("mix", dp, 0)
                vscaled("mix", dt, 0, rv[:, :])
                split("mix", dp, 1)
                ts(rg[:, :], rv[:, :], cols[:, COL["k_norm"]:COL["k_norm"] + 1], None, ALU.mult, None,
                   [(tile_scaled, scaled("mix", dt, 0))], kv_v.done("g"))
                split("mix", dp, 2)
                vscaled("mix", dt, 1, va[:, :])
                split("mix", dp, 3)
                rope(kv_v, kv_a, kv_p, "k_norm", j, k_r[:, :], "k")
                dve.wait_ge(kv_p.sem, kv_p.at("v", j))
                nc.vector.tensor_copy(va_tok[:, :, :], psV[:, 0:2 * P].rearrange("p (b q) -> p b q", b=2))\
                    .then_inc(*kv_v.done("vtok"))
                with nc.vector.Fori(0, 4) as i:
                    m = j * 4 + i
                    dp, dt = j * 36 + i * 8, j * 18 + i * 4
                    V = lambda name: (b2_v.sem, b2_v.at(name, m))
                    split("mix", dp, 4)
                    vscaled("mix", dt, 2, rv[:, :])
                    split("mix", dp, 5)
                    ts(rg[:, :], rv[:, :], cols[:, COL["q_norm"]:COL["q_norm"] + 1], None, ALU.mult, None,
                       [(tile_scaled, scaled("mix", dt, 2))], b2_v.done("g"))
                    split("mix", dp, 6)
                    vscaled("mix", dt, 3, kb[:, :])
                    split("mix", dp, 7)
                    rope(b2_v, b2_a, b2_p, "q_norm", m, q_r[:, :], "q")
                    split("mix", dp, 8)
                    vscaled("mix", dt, 4, qb[:, :])
                    split("mix", dp, 9)
                    dve.wait_ge(b2_p.sem, b2_p.at("scoresA", m))
                    nc.vector.tensor_reduce(stA[:, 0:2], psS[:, :, :], AX.X, ALU.max).then_inc(*b2_v.done("maxA"))
                    ts(stA[:, 2:4], stA[:, 0:2], -SCALE, None, ALU.mult, None, [V("maxA")], b2_v.done("nmaxA"))
                    dve.wait_ge(b2_a.sem, b2_a.at("e1A", m))
                    nc.vector.reciprocal(stA[:, 6:8], stA[:, 4:6]).then_inc(*b2_v.done("recipA"))
                    for b in range(2):
                        ts(pA[:, b, :], pA[:, b, :], stA[:, 6 + b:7 + b], None, ALU.mult, None, [V("recipA")],
                           b2_v.done(f"p{b}A"))
                    stt(sB[:, :, :], psF[:, :, :], SCALE, rbm[:, :, :], ALU.mult, ALU.add,
                        [(b2_p.sem, b2_p.at("scoresB", m)), (b2_g.sem, b2_g.at("rbm", m))], b2_v.done("sB"))
                    dve.wait_ge(*V("sB"))
                    nc.vector.tensor_reduce(stB[:, 0:2], sB[:, :, :], AX.X, ALU.max).then_inc(*b2_v.done("maxB"))
                    ts(stB[:, 2:4], stB[:, 0:2], -1.0, None, ALU.mult, None, [V("maxB")], b2_v.done("nmaxB"))
                    split("mix", dp, 10)
                    dve.wait_ge(b2_a.sem, b2_a.at("e1B", m))
                    nc.vector.reciprocal(stB[:, 6:8], stB[:, 4:6]).then_inc(*b2_v.done("recipB"))
                    for b in range(2):
                        ts(pB[:, b, :], pB[:, b, :], stB[:, 6 + b:7 + b], None, ALU.mult, None, [V("recipB")],
                           b2_v.done(f"p{b}B"))
                    vscaled("mix", dt, 5, vb[:, :])
                    split("mix", dp, 11)
                    dve.wait_ge(b2_p.sem, b2_p.at("vTB", m))
                    nc.vector.tensor_copy(vb_tok[:, :, :], psV[:, 0:2 * P].rearrange("p (b q) -> p b q", b=2))\
                        .then_inc(*b2_v.done("vtokB"))
                    tt(mixed[:, m, T:2 * T], psO[:, 0:T], mixed[:, m, 0:T].bitcast(F32), ALU.subtract,
                       [(b2_a.sem, b2_a.at("highA", m))], b2_v.done("lowA"))
                    tt(mixed[:, m + 8, T:2 * T], psN[:, 0:T], mixed[:, m + 8, 0:T].bitcast(F32), ALU.subtract,
                       [(b2_a.sem, b2_a.at("highB", m))], b2_v.done("lowB"))
                    for b in range(2):
                        c = m * 2 + b
                        stt(x[:, c, :], x[:, c, :], col("g_final", c), rstd_x[:, :], ALU.mult, ALU.mult,
                            [], (x_final, 1))

            with nc.vector.Fori(0, 8) as i:
                for b in range(2):
                    split("wo", i * 4, 2 * b)
                    vsum("wo", i * 2, b, tsum[:, b, :])
                    split("wo", i * 4, 2 * b + 1)

            def updated(n, before, src, scaled_before, g, added):
                norm_rstd(dve, before, rstd_x)
                with nc.vector.Fori(0, 8) as i:
                    for b in range(2):
                        c = i * 2 + b
                        tt(x[:, c, :], x[:, c, :], src[:, c, :], ALU.add,
                           [(post_scaled, i * 2 + (scaled_before + b + 1))], (added, 1))
                    for b in range(2):
                        h_low(dve, n, i, b, col(g, i * 2 + b))
                norm_rstd(dve, n)

            updated(norms["mlp2"], norms["mixed2"], mix32, 0, "pre_mlp", x_mixed)
            link(nc.vector.memset(acc[:, :, :], 0.0))
            with nc.vector.Fori(0, 2) as j:
                with nc.vector.Fori(0, 16) as i:
                    dp, dt = j * 128 + i * 4, j * 48 + i * 2
                    for b in range(2):
                        m = j * 32 + i * 2 + b
                        split("mlp", dp, 2 * b)
                        vscaled("mlp", dt, b, tsum[:, b, :], None)
                        stt(tmp[:, b, :], tsum[:, b, :], 0.0, tsum[:, b, :], ALU.max, ALU.mult,
                            [(tile_scaled, scaled("mlp", j * 32 + i * 2, b))], sq_v.done("sq"))
                        split("mlp", dp, 2 * b + 1)
                        tt(hidden2[:, i * 2 + b, T:2 * T], tmp[:, b, :], hidden2[:, i * 2 + b, 0:T].bitcast(F32),
                           ALU.subtract, [(sq_a.sem, sq_a.at("high", m))], sq_v.done("low"))
                with nc.vector.Fori(0, 8) as i:
                    dp, dt = j * 128 + i * 8, j * 48 + i * 2
                    for k in range(8):
                        if k % 4 == 3:
                            b = k // 4
                            vsum("mlp", dt, 32 + b, tsum[:, b, :])
                            tt(acc[:, i * 2 + b, :], acc[:, i * 2 + b, :], tsum[:, b, :], ALU.add,
                               [(tile_summed, summed("mlp", dt, 32 + b))], (acc_added, 1))
                        split("mlp", dp, 64 + k)
            tt(p_hl[:, :, T:2 * T], p_raw[:, :, :], p_hl[:, :, 0:T].bitcast(F32), ALU.subtract,
               [(p_split, 1)], (p_split, 1))
            for t in range(16):
                vsum("ple", 0, t, e[:, t, :])
                if t % 4 == 3:
                    split("ple", 0, t // 4)
            updated(norms["ple2"], norms["mlped2"], acc, KD, "pre_ple", x_mlped)

            def embed(i, last):
                for b in range(2):
                    if not last:
                        split("ple_gate", i * 4, 2 * b)
                    vscaled("ple_gate", i * 2, b, tsum[:, b, :])
                    if not last:
                        split("ple_gate", i * 4, 2 * b + 1)
                    tt(e[:, i * 2 + b, :], e[:, i * 2 + b, :], tmp[:, b, :], ALU.mult,
                       [(ple_a, i * 2 + (b + 1))], (ple_v, 1))

            with nc.vector.Fori(0, 7) as i:
                embed(i, False)
            embed(7, True)
            norm_rstd(dve, norms["pled2"], rstd_x)
            dve.wait_ge(norms["pled2"].rstd, 1)
            for c in range(RESULT_V):
                tt(e[:, c, :], e[:, c, :], rstd_x[:, :], ALU.mult, [], (result_t, 1))
                tt(x[:, c, :], x[:, c, :], e[:, c, :], ALU.add, [(result_t, c + 1)], (result_v, 1))

        @block.tensor
        def _(pe):
            mm = nc.tensor.matmul

            def tile(stage, dp, dt, t, first_piece, rhs, chunks=KD, norm=None):
                tile_matmuls(pe, stage, dp, dt, t, first_piece * BLOCKS, chunks, rhs, norm)

            def transposed(dst, src):
                return nc.tensor.transpose(dst, src, ident[:, :])

            pe.wait_ge(vector_chain, 2)
            pe.wait_ge(const_landed, 32)
            norm_tensor(pe, norms["mix1"])
            with nc.tensor.Fori(0, 8) as i:
                dp, dt = i * 8, i * 4
                tile("rnn", dp, dt, 0, 0, h_chunk, norm=norms["mix1"])
                tile("rnn", dp, dt, 1, 2, h_chunk)
                pe.wait_ge(wgate_landed, i * 16 + 16)
                pe.wait_ge(rnn_v.sem, rnn_v.at("u", i))
                mm(psS[:, 0, :], wgate[:, 0:P], u[:, :], start=True, stop=True)
                mm(psS[:, 1, :], wgate[:, P:2 * P], u[:, :], start=True, stop=True).then_inc(*rnn_p.done("gates"))
                tile("rnn", dp, dt, 2, 4, h_chunk)
                tile("rnn", dp, dt, 3, 6, h_chunk)
            tile("forget", 0, 0, 0, 0, h_chunk)

            def branch(stage, ready):
                pe.wait_ge(*ready)
                with nc.tensor.Fori(0, 4) as i:
                    for t in range(4):
                        tile(stage, i * 4, i * 4, t, t, y_chunk, chunks=8)

            branch("rnn_branch", (rnn_v.sem, rnn_v.at("low", 7)))
            pe.wait_ge(vector_chain, F_STEPS)
            for b in range(2):
                last = transposed(psV[:, b * P:(b + 1) * P], fcum[:, b * P:(b + 1) * P])
            last.then_inc(*forget_p.done("FT"))

            with nc.tensor.Fori(0, 8) as i:
                dp, dt = i * 12, i * 6
                for t in range(3):
                    tile("attn", dp, dt, t, 2 * t, h_chunk)
                pe.wait_ge(tile_scaled, scaled("attn", dt, 1))
                for b in range(2):
                    last = mm(psS[:, b, :], qT[:, b * P:(b + 1) * P], kT[:, :], start=True, stop=True)
                last.then_inc(*att_p.done("scores"))
                pe.wait_ge(att_v.sem, att_v.at("fsel", i))
                mm(psF[:, 0, :], ones[:, :], fsel[:, :], start=True, stop=True).then_inc(*att_p.done("fk"))
                tile("attn", dp, dt, 3, 6, h_chunk)
                pe.wait_ge(tile_scaled, scaled("attn", dt, 2))
                for b in range(2):
                    last = transposed(psV[:, b * P:(b + 1) * P], vT[:, b * P:(b + 1) * P])
                last.then_inc(*att_p.done("vT"))
                tile("attn", dp, dt, 4, 8, h_chunk)
                pe.wait_ge(att_v.sem, att_v.at("p1", i))
                for b in range(2):
                    for kb_ in range(2):
                        last = transposed(psT[:, kb_, b * P:(b + 1) * P], pr[:, b, kb_ * P:(kb_ + 1) * P])
                last.then_inc(*att_p.done("pT"))
                tile("attn", dp, dt, 5, 10, h_chunk)
                pe.wait_ge(att_a.sem, att_a.at("prT", i))
                pe.wait_ge(att_v.sem, att_v.at("vtok", i))
                for b in range(2):
                    last = mm(psO[:, 0:T], vtok[:, b, :], prT[:, b, :], start=b == 0, stop=b == 1)
                last.then_inc(*att_p.done("out"))
            branch("attn_branch", (att_v.sem, att_v.at("low", 7)))

            with nc.tensor.Fori(0, 8) as i:
                for b in range(2):
                    tile("pool", i * 4, i * 2, b, 2 * b, h_chunk)
            pe.wait_ge(const3_landed, 32)
            for g in range(4):
                pe.wait_ge(pooled_done, POOLED[g])
                if g == 3:
                    pe.wait_ge(pool_a.sem, pool_a.at("s1"))
                bank = (psS, psF, psT)[g % 3]
                for m in range(2):
                    for c in range(2):
                        last = mm(bank[:, m, :], wpool[:, g, c, m * P:(m + 1) * P], pooled[:, 2 * g + c, :],
                                  start=c == 0, stop=c == 1)
                last.then_inc(*pool_p.done(f"y{g}"))
            branch("pool_branch", (pool_v.sem, pool_v.at("l7")))

            pe.wait_ge(merged_v.sem, merged_v.at("low1"))
            with nc.tensor.Fori(0, 8) as i:
                for b in range(2):
                    tile("out", i * 4, i * 2, b, 2 * b, merged_chunk)
            norm_tensor(pe, norms["ffn1"])
            with nc.tensor.Fori(0, KF) as i:
                for b in range(2):
                    tile("up", i * 4, i * 2, b, 2 * b, h_chunk, norm=None if b else norms["ffn1"])
            pe.wait_ge(up_v.sem, up_v.at("low", KF - 1))
            with nc.tensor.Fori(0, 2) as i:
                for t in range(8):
                    tile_matmuls(pe, "down", i * KF, i * 8, t, t * KF, KF, lambda c: hidden[:, c, :])
            norm_tensor(pe, norms["final"])
            norm_tensor(pe, norms["mix2"], total_g, 1)

            pe.wait_ge(const4_landed, 64)

            def turned(square, steps):
                pe.wait_ge(*square)
                mm(psN[:, 0:T], ones[:, :], rsq[:, :], start=True, stop=True).then_inc(*steps.done("stat"))

            with nc.tensor.Fori(0, 2) as j:
                tile("mix", j * 36, j * 18, 0, 0, h_chunk, norm=norms["mix2"])
                tile("mix", j * 36, j * 18, 1, 2, h_chunk)
                turned((kv_a.sem, kv_a.at("square", j)), kv_p)
                pe.wait_ge(kv_v.sem, kv_v.at("g", j))
                mm(psN[:, T:2 * T], turn[:, :], rg[:, :], start=True, stop=True).then_inc(*kv_p.done("turn"))
                pe.wait_ge(tile_scaled, scaled("mix", j * 18, 1))
                for b in range(2):
                    last = transposed(psV[:, b * P:(b + 1) * P], va[:, b * P:(b + 1) * P])
                last.then_inc(*kv_p.done("v"))
                with nc.tensor.Fori(0, 4) as i:
                    m = j * 4 + i
                    dp, dt = j * 36 + i * 8, j * 18 + i * 4
                    tile("mix", dp, dt, 2, 4, h_chunk)
                    tile("mix", dp, dt, 3, 6, h_chunk)
                    turned((b2_a.sem, b2_a.at("square", m)), b2_p)
                    pe.wait_ge(b2_v.sem, b2_v.at("g", m))
                    mm(psN[:, T:2 * T], turn[:, :], rg[:, :], start=True, stop=True).then_inc(*b2_p.done("turn"))
                    tile("mix", dp, dt, 4, 8, h_chunk)
                    pe.wait_ge(b2_v.sem, b2_v.at("q", m))
                    for b in range(2):
                        last = mm(psS[:, b, :], q_r[:, b * P:(b + 1) * P], k_r[:, :], start=True, stop=True)
                    last.then_inc(*b2_p.done("scoresA"))
                    pe.wait_ge(tile_scaled, scaled("mix", dt, 4))
                    for b in range(2):
                        last = mm(psF[:, b, :], qb[:, b * P:(b + 1) * P], kb[:, :], start=True, stop=True)
                    last.then_inc(*b2_p.done("scoresB"))
                    tile("mix", dp, dt, 5, 10, h_chunk)
                    pe.wait_ge(b2_v.sem, b2_v.at("p1A", m))
                    for b in range(2):
                        for kb_ in range(2):
                            last = transposed(psT[:, kb_, b * P:(b + 1) * P], pA[:, b, kb_ * P:(kb_ + 1) * P])
                    last.then_inc(*b2_p.done("pTA"))
                    pe.wait_ge(b2_v.sem, b2_v.at("p1B", m))
                    for b in range(2):
                        for kb_ in range(2):
                            last = transposed(psS[:, kb_, b * P:(b + 1) * P], pB[:, b, kb_ * P:(kb_ + 1) * P])
                    last.then_inc(*b2_p.done("pTB"))
                    pe.wait_ge(tile_scaled, scaled("mix", dt, 5))
                    for b in range(2):
                        last = transposed(psV[:, b * P:(b + 1) * P], vb[:, b * P:(b + 1) * P])
                    last.then_inc(*b2_p.done("vTB"))
                    pe.wait_ge(b2_a.sem, b2_a.at("pAT", m))
                    for b in range(2):
                        last = mm(psO[:, 0:T], va_tok[:, b, :], pAT[:, b, :], start=b == 0, stop=b == 1)
                    last.then_inc(*b2_p.done("outA"))
                    pe.wait_ge(b2_a.sem, b2_a.at("pBT", m))
                    pe.wait_ge(b2_v.sem, b2_v.at("vtokB", m))
                    for b in range(2):
                        last = mm(psN[:, 0:T], vb_tok[:, b, :], pBT[:, b, :], start=b == 0, stop=b == 1)
                    last.then_inc(*b2_p.done("outB"))

            pe.wait_ge(b2_v.sem, b2_v.at("lowB", 7))
            with nc.tensor.Fori(0, 8) as i:
                for b in range(2):
                    tile("wo", i * 4, i * 2, b, 2 * b, lambda c: mixed[:, c, :])
            norm_tensor(pe, norms["mixed2"])
            norm_tensor(pe, norms["mlp2"])
            with nc.tensor.Fori(0, 2) as j:
                with nc.tensor.Fori(0, 16) as i:
                    for b in range(2):
                        tile("mlp", j * 128 + i * 4, j * 48 + i * 2, b, 2 * b, h_chunk,
                             norm=None if b else norms["mlp2"])
                with nc.tensor.Fori(0, 8) as i:
                    pe.wait_ge(sq_v.sem, sq_v.at("low", j * 32 + 31))
                    for b in range(2):
                        tile("mlp", j * 128 + i * 8, j * 48 + i * 2, 32 + b, 64 + 4 * b,
                             lambda c: hidden2[:, c, :], chunks=32)
            pe.wait_ge(p_split, 2)
            for t in range(16):
                tile_matmuls(pe, "ple", 0, 0, t, 2 * t, 2, lambda c: p_hl[:, c, :], tile_sem=ple_tile_done)
            norm_tensor(pe, norms["mlped2"])
            norm_tensor(pe, norms["ple2"])
            with nc.tensor.Fori(0, 8) as i:
                for b in range(2):
                    tile("ple_gate", i * 4, i * 2, b, 2 * b, h_chunk, norm=None if b else norms["ple2"])
            norm_tensor(pe, norms["pled2"])


DOWN_ENDS = {}
for _t in range(8):
    DOWN_ENDS.setdefault(((_t + 1) * KF - 1) // BLOCKS, []).append(_t)

RESULT_V = 11

LOG_SIGMOID_STEPS = 2 + 5 + 8 + 1 + 2
LS_STEPS = 3 + 1 + LOG_SIGMOID_STEPS
F_STEPS = LS_STEPS + 1 + LOG_SIGMOID_STEPS + 2
POOLED = [1 + sum(k + 1 + 3 for k in range(g + 1)) for g in range(4)]


def _stream(inputs):
    import numpy as np

    def blocks(m):
        k, o = m.shape
        return m.reshape(k // P, P, o // P, P).transpose(2, 0, 1, 3)

    W = {k: np.asarray(v)[0] for k, v in inputs.items() if k.startswith("w_")}
    w_in, out = W["w_in"], []

    def put(b):
        out.append(b.reshape(-1, P, P))

    o = 0
    where = {}
    for name, width in (("rx", 1024), ("ry", 1024), ("q", 1024), ("k", 1024), ("v", 1024), ("f", 8), ("pool", 1024),
                        ("gate", 6144)):
        where[name] = o
        o += width

    def part(name, tile):
        c = where[name] + tile * P
        return blocks(w_in[:, c:c + P])

    for i in range(8):
        put(part("rx", i)), put(part("ry", i)), put(part("gate", 2 * i)), put(part("gate", 2 * i + 1))
    put(part("f", 0))
    put(blocks(W["w_branch_rnn"]))
    for i in range(8):
        for name in ("q", "k", "v", "pool"):
            put(part(name, i))
        put(part("gate", 16 + 2 * i)), put(part("gate", 17 + 2 * i))
    put(blocks(W["w_branch_attn"]))
    for i in range(16):
        put(part("gate", 32 + i))
    put(blocks(W["w_branch_pool"]))
    put(blocks(W["w_out"]))
    gate_up = blocks(W["w_ffn_in"])
    for i in range(KF):
        put(gate_up[i]), put(gate_up[KF + i])
    put(blocks(W["w_ffn_out"]))
    in2 = blocks(W["w_in_2"])
    for j in range(2):
        put(in2[8 + j]), put(in2[10 + j])
        for i in range(4 * j, 4 * j + 4):
            put(in2[i]), put(in2[20 + i]), put(in2[12 + i]), put(in2[28 + i])
    put(blocks(W["w_o_2"]))
    up, down = blocks(W["w_up_2"]), blocks(W["w_down_2"])
    for half in range(2):
        put(up[32 * half:32 * half + 32]), put(down[:, 32 * half:32 * half + 32])
    put(blocks(W["w_ple_proj_2"])), put(blocks(W["w_ple_gate_2"]))
    flat = np.concatenate(out)
    assert len(flat) == PIECES * BLOCKS
    groups = -(-PIECES // RING)
    stream = np.empty((groups * RING, P, BLOCKS, P), flat.dtype)
    stream[:PIECES] = flat.reshape(PIECES, BLOCKS, P, P).transpose(0, 2, 1, 3)
    stream[PIECES:] = 0
    return stream.reshape(groups, RING, P, PIECE)


def _tables():
    import numpy as np
    far = np.float32(-1e30)
    q = np.arange(T)
    causal = np.where(q[:, None] >= q[None, :], np.float32(0), far)
    c = q % 64
    c0 = np.clip(c - 8, 0, 48)
    near = np.where((c[None, :] >= c0[:, None]) & (c[None, :] < c0[:, None] + 16), np.float32(0), far)

    def by_query(m):
        return np.ascontiguousarray(m.reshape(2, P, T).transpose(1, 0, 2))

    freqs = np.float32(10000.0) ** (-np.arange(32, dtype=np.float32) / 32)
    angle = np.empty((P, T), np.float32)
    turn = np.zeros((P, P), np.float32)
    for axis, pos in ((0, q // 64), (1, q % 64)):
        for half in range(2):
            d = 64 * axis + 32 * half
            angle[d:d + 32] = freqs[:, None] * pos.astype(np.float32)[None, :]
            for n in range(32):
                turn[64 * axis + 32 * (1 - half) + n, d + n] = 1.0 if half else -1.0
    inv = np.stack([1.0 / np.minimum(np.arange(1, T + 1), wdw) for wdw in (2, 4, 8, 16)]).astype(np.float32)
    return {
        "causal_mask": by_query(causal), "near_mask": by_query(near), "rope_cos": np.cos(angle),
        "rope_sin": np.sin(angle), "rope_turn": turn,
        "inv_count": np.ascontiguousarray(np.broadcast_to(inv, (P, 4, T))), "unit": np.eye(P, dtype=np.float32),
    }


def _arrays(inputs):
    import numpy as np
    A = {k: np.asarray(v) for k, v in inputs.items()}

    def chunks(v):
        return v.reshape(-1, P).T

    cols = np.zeros((P, NCOL), np.float32)
    for name, v in (("g_mix", A["g_mix"]), ("g_ffn", A["g_ffn"]), ("g_final", A["g_final"]),
                    ("pre_mix", A["pre_mix_norm_2"]), ("post_mix", A["post_mix_norm_2"]),
                    ("pre_mlp", A["pre_mlp_norm_2"]), ("post_mlp", A["post_mlp_norm_2"]),
                    ("pre_ple", A["pre_ple_norm_2"]), ("post_ple", A["post_ple_norm_2"]),
                    ("conv0", A["conv_w"][0, 0]), ("conv1", A["conv_w"][0, 1]), ("conv2", A["conv_w"][0, 2]),
                    ("conv3", A["conv_w"][0, 3]), ("conv_b", A["conv_b"]), ("b_rg", A["b_rg"]), ("b_ig", A["b_ig"]),
                    ("lam", A["lru_lambda"]), ("pool_scale", A["pool_scale"]), ("q_norm", A["q_norm_2"]),
                    ("k_norm", A["k_norm_2"])):
        c = chunks(v)
        cols[:, COL[name]:COL[name] + c.shape[1]] = c
    cols[:HEADS, COL["b_forget"]] = A["b_forget"][0]
    q = np.arange(T)
    row, column = q // 64, q % 64
    dr = row[None, :] - row[:, None] + 7
    dc = np.clip(column[None, :] - column[:, None] + 15, 0, 30)
    rel = A["rel_pos_bias_2"][0][:, dr, dc]
    return {
        "w": _stream(A),
        "xT": np.ascontiguousarray(A["x"][0].T.reshape(KD, P, T).transpose(1, 0, 2)),
        "pT": np.ascontiguousarray(A["p_2"][0, 0].T.reshape(2, P, T).transpose(1, 0, 2)),
        "columns": cols,
        "w_gates": np.ascontiguousarray(np.concatenate([A["w_rg"][0], A["w_ig"][0]], axis=2)),
        "w_pool": np.ascontiguousarray(A["w_pool"][0].reshape(4, 2, P, 2 * P).transpose(2, 0, 1, 3)),
        "rel_bias": np.ascontiguousarray(rel.reshape(HEADS, 2, P, T).transpose(0, 2, 1, 3)),
        **_tables(),
    }


_ORDER = ["w", "xT", "pT", "columns", "w_gates", "w_pool", "rel_bias", "near_mask", "causal_mask", "rope_cos",
          "rope_sin", "rope_turn", "inv_count", "unit"]


def kernel(**inputs):
    import numpy as np
    import concourse.bacc as _bacc
    from concourse import mybir as _mybir
    from concourse.bass_utils import run_bass_kernel_spmd as _run

    nc = _bacc.Bacc("TRN2", target_bir_lowering=False, num_devices=1)
    arrays = _arrays(inputs)
    args = [nc.dram_tensor(n, arrays[n].shape, _mybir.dt.from_np(arrays[n].dtype), kind="ExternalInput").ap()
            for n in _ORDER]
    out = nc.dram_tensor("outT", (P, KD, T), F32, kind="ExternalOutput").ap()
    build(nc, *args, out)
    r = _run(nc, [arrays], core_ids=[0])
    got = r.results[0]["outT"]
    return np.ascontiguousarray(np.asarray(got).transpose(2, 1, 0).reshape(1, T, D))
```

```python
import math
from contextlib import ExitStack

import concourse.bass as bass
from concourse import mybir

F32 = mybir.dt.float32
F32R = mybir.dt.float32r
ALU = mybir.AluOpType
ACT = mybir.ActivationFunctionType
AX = mybir.AxisListType
ds = bass.ds

P = 128
T = 256
D = 2048
KD = D // P
D_RNN = 1024
HEADS = 8
D_FF = 5632
KF = D_FF // P
D_FF2 = 8192
EPS = 1e-6
SCALE = 128 ** -0.5
RING = 4
BLOCKS = 8
GATES_AT = 10
PIECE = BLOCKS * P
EARLY = 8
POOLED_AFTER = 5

STAGE_LIST = [
    ("rnn", 8 * 8, 8 * 4, 8 * 4),
    ("forget", 2, 1, 1),
    ("rnn_branch", 16, 16, 0),
    ("attn", 8 * 12, 8 * 6, 8 * 6),
    ("attn_branch", 16, 16, 0),
    ("pool", 16 * 2, 16, 16),
    ("pool_branch", 16, 16, 0),
    ("out", 32, 16, 0),
    ("up", 2 * 2 * KF, 2 * KF, 2 * KF),
    ("down", 2 * KF, 16, 0),
    ("mix", 2 * 36, 36, 36),
    ("wo", 32, 16, 0),
    ("mlp", 2 * (64 + 64), 2 * (32 + 16), 2 * 32),
    ("ple", 4, 16, 0),
    ("ple_gate", 32, 16, 16),
]


class Stage:

    def __init__(self, piece, tile, scaled):
        self.piece, self.tile, self.scaled = piece, tile, scaled


def plan():
    stages, piece, tile, scaled = {}, 0, 0, 0
    for name, pieces, tiles, normed in STAGE_LIST:
        stages[name] = Stage(piece, tile, scaled)
        piece, tile, scaled = piece + pieces, tile + tiles, scaled + normed
    return stages, piece


STAGES, PIECES = plan()

COLUMN_LIST = [
    ("g_mix", 16), ("g_ffn", 16), ("g_final", 16), ("pre_mix", 16), ("post_mix", 16),
    ("pre_mlp", 16), ("post_mlp", 16), ("pre_ple", 16), ("post_ple", 16),
    ("conv0", 8), ("conv1", 8), ("conv2", 8), ("conv3", 8), ("conv_b", 8),
    ("b_rg", 8), ("b_ig", 8), ("lam", 8), ("pool_scale", 8), ("b_forget", 1), ("q_norm", 1), ("k_norm", 1),
]
COL, NCOL = {}, 0
for _name, _n in COLUMN_LIST:
    COL[_name] = NCOL
    NCOL += _n


class Steps:

    def __init__(self, sem, names):
        self.sem, self.names, self.next = sem, names.split(), 0

    def done(self, name):
        assert self.names[self.next % len(self.names)] == name, (name, self.names, self.next)
        self.next += 1
        return self.sem, 1

    def at(self, name, i=0):
        return i * len(self.names) + self.names.index(name) + 1


def build(nc, w, xT, pT, columns, w_gates, w_pool, rel_bias, near_mask, causal_mask, rope_cos,
          rope_sin, rope_turn, inv_count, unit, outT):
    ctx = ExitStack()
    with ctx:
        def sem(name):
            return ctx.enter_context(nc.semaphore(name))

        SBUF_TOP = nc.sbuf_usable_end
        base = (nc.sbuf_base + 63) // 64 * 64

        def size(shape):
            n = 4
            for s in shape[1:]:
                n *= s
            return -(-n // 64) * 64

        class Area:
            def __init__(self, start, end):
                self.start, self.next, self.end = start, start, end

            def put(self, name, shape, dt=F32):
                t = nc.alloc_sbuf_tensor_at(name, shape, dt, offset=self.next)
                self.next += size(shape)
                assert self.next <= self.end, (name, self.next, self.end)
                return t

        whole = Area(base, SBUF_TOP)
        raw = whole.put("w_raw", [P, RING, PIECE])
        w_hi = whole.put("w_hi", [P, RING, PIECE], F32R)
        w_lo = whole.put("w_lo", [P, RING, PIECE], F32R)
        x = whole.put("x", [P, KD, T])
        h_at = whole.next
        h = whole.put("h", [P, KD, 2 * T], F32R)
        region = whole.next
        REGION = KF * 2 * T * 4
        whole.next += REGION
        low = whole.put("low", [P, 2, T])
        tsum = whole.put("tsum", [P, 2, T])
        tmp = whole.put("tmp", [P, 2, T])
        sq2 = whole.put("sq2", [P, 2, T])
        sqg2 = whole.put("sqg2", [P, 2, T])
        rstd = whole.put("rstd", [P, T])
        rstd_x = whole.put("rstd_x", [P, T])
        root = whole.put("root", [P, T])
        total = whole.put("total", [P, T])
        total_g = whole.put("total_g", [P, T])
        cols = whole.put("cols", [P, NCOL])
        g_both = whole.put("g_both", [P, KD])
        eps = whole.put("eps", [P, 1])
        decay = whole.put("decay", [P, 8])
        ones = whole.put("ones", [P, P])
        ident = whole.put("ident", [P, P])

        def col(name, i=0):
            return cols[:, ds(i + COL[name], 1)]

        a1 = Area(region, region + REGION)
        gate = a1.put("gate", [P, KD, T])
        merged = a1.put("merged", [P, KD, T])
        y = a1.put("y", [P, 8, 2 * T], F32R)
        PADT = 16 + T
        pool_x = a1.put("pool_x", [P, 8, PADT])
        mixers1 = a1.next
        merged_hl = Area(region + 48 * 1024, region + REGION).put("merged_hl", [P, KD, 2 * T], F32R)
        a_rnn = Area(mixers1, region + REGION)
        wgate = a_rnn.put("wgate", [P, 2 * P])
        rx = a_rnn.put("rx", [P, 4 + T])
        u = a_rnn.put("u", [P, T])
        ry = a_rnn.put("ry", [P, T])
        r_g = a_rnn.put("r_g", [P, T])
        i_g = a_rnn.put("i_g", [P, T])
        a_t = a_rnn.put("a_t", [P, T])
        th = a_rnn.put("th", [P, T])
        a2 = a_rnn.put("a2", [P, T])
        gap = a_rnn.put("gap", [P, T])
        sq = a_rnn.put("sq", [P, T])
        iu = a_rnn.put("iu", [P, T])
        b_in = a_rnn.put("b_in", [P, T])
        hid = a_rnn.put("hid", [P, T])
        y2 = a_rnn.put("y2", [P, T])
        y3 = a_rnn.put("y3", [P, T])
        inner = a_rnn.put("inner", [P, T])
        sg = a_rnn.put("sg", [P, T])
        gl = a_rnn.put("gl", [P, T])
        y_r = a_rnn.put("y_r", [P, T])
        ls = a_rnn.put("ls", [P, 8, 8])
        a_att = Area(mixers1, region + REGION)
        fl = a_att.put("fl", [P, T])
        fcum = a_att.put("fcum", [P, T])
        f_t = a_att.put("f_t", [P, 2, P])
        fsel = a_att.put("fsel", [P, T])
        cmask = a_att.put("cmask", [P, 2, T])
        fl_at = a_att.next
        qT = a_att.put("qT", [P, T])
        kT = a_att.put("kT", [P, T])
        vT = a_att.put("vT", [P, T])
        bias = a_att.put("bias", [P, 2, T])
        biasm = a_att.put("biasm", [P, 2, T])
        sc = a_att.put("sc", [P, 2, T])
        pr = a_att.put("pr", [P, 2, T])
        prT = a_att.put("prT", [P, 2, T])
        vtok = a_att.put("vtok", [P, 2, P])
        st = a_att.put("st", [P, 8])
        lf = Area(fl_at, region + REGION).put("lf", [P, 8, T])
        a_pool = Area(mixers1, region + REGION)
        sums = a_pool.put("sums", [P, 2, 2, PADT])
        pooled = a_pool.put("pooled", [P, 8, T])
        inv = a_pool.put("inv", [P, 4, T])
        wpool = a_pool.put("wpool", [P, 4, 2, 2 * P])
        hidden = Area(region, region + REGION).put("hidden", [P, KF, 2 * T], F32R)

        a2_ = Area(region, region + REGION)
        mixed = a2_.put("mixed", [P, 16, 2 * T], F32R)
        mix32 = a2_.put("mix32", [P, KD, T])
        cos_t = a2_.put("cos_t", [P, T])
        sin_t = a2_.put("sin_t", [P, T])
        nmask = a2_.put("nmask", [P, 2, T])
        turn = a2_.put("turn", [P, P])
        rbias = a2_.put("rbias", [P, 2, T])
        rbm = a2_.put("rbm", [P, 2, T])
        rv = a2_.put("rv", [P, T])
        rrs = a2_.put("rrs", [P, T])
        rsq = a2_.put("rsq", [P, T])
        rg = a2_.put("rg", [P, T])
        rcos = a2_.put("rcos", [P, T])
        rsin = a2_.put("rsin", [P, T])
        rsum = a2_.put("rsum", [P, T])
        q_r = a2_.put("q_r", [P, T])
        k_r = a2_.put("k_r", [P, T])
        va = a2_.put("va", [P, T])
        va_tok = a2_.put("va_tok", [P, 2, P])
        qb = a2_.put("qb", [P, T])
        kb = a2_.put("kb", [P, T])
        vb = a2_.put("vb", [P, T])
        vb_tok = a2_.put("vb_tok", [P, 2, P])
        sB = a2_.put("sB", [P, 2, T])
        pA = a2_.put("pA", [P, 2, T])
        pAT = a2_.put("pAT", [P, 2, T])
        pB = a2_.put("pB", [P, 2, T])
        pBT = a2_.put("pBT", [P, 2, T])
        stA = a2_.put("stA", [P, 8])
        stB = a2_.put("stB", [P, 8])
        a3 = Area(region, region + REGION)
        hidden2 = a3.put("hidden2", [P, 32, 2 * T], F32R)
        acc = a3.put("acc", [P, KD, T])
        p_raw = a3.put("p_raw", [P, 2, T])
        p_hl = a3.put("p_hl", [P, 2, 2 * T], F32R)
        e = Area(region, region + REGION).put("e", [P, KD, T])

        ps = [ctx.enter_context(nc.psum_tensor(f"ps_tile{b}", [P, 2 * T], F32)) for b in range(2)]
        psN = ctx.enter_context(nc.psum_tensor("psN", [P, 2 * T], F32))
        psS = ctx.enter_context(nc.psum_tensor("psS", [P, 2, T], F32))
        psF = ctx.enter_context(nc.psum_tensor("psF", [P, 2, T], F32))
        psT = ctx.enter_context(nc.psum_tensor("psT", [P, 2, T], F32))
        psV = ctx.enter_context(nc.psum_tensor("psV", [P, 2 * T], F32))
        psO = ctx.enter_context(nc.psum_tensor("psO", [P, 2 * T], F32))

        landed = [sem(f"piece_landed{r}") for r in range(RING)]
        hi_ready = sem("hi_ready")
        split_done = sem("split_done")
        piece_used = sem("piece_used")
        low_copied = sem("low_copied")
        tile_summed = sem("tile_summed")
        ple_tile_done = sem("ple_tile_done")
        tile_scaled = sem("tile_scaled")
        g_both_ready = sem("g_both_ready")
        squared_mix = sem("squared_mix")
        post_scaled = sem("post_scaled")
        mix_gained = sem("mix_gained")
        e_gained = sem("e_gained")
        columns_landed = sem("columns_landed")
        unit_landed = sem("unit_landed")
        vector_chain = sem("vector_chain")
        scalar_chain = sem("scalar_chain")

        def S(names, label):
            return Steps(sem(label), names)

        def four_squares(c):
            return (sq2, sqg2)[c % 4 // 2][:, c % 2, :]

        def tile_matmuls(pe, stage, dp, dt, tile, first_block, chunks, rhs, norm=None, tile_sem=None, between=None,
                         ready=None):
            st_ = STAGES[stage]
            bank = ps[(st_.tile + tile) % 2]
            pe.wait_ge(tile_summed, dt + (st_.tile + tile + 1))
            for c in range(chunks):
                q = first_block + c
                if q % BLOCKS == 0 or c == 0:
                    pe.wait_ge(split_done, dp + (st_.piece + q // BLOCKS + 1))
                if between and c in between:
                    between[c]()
                slot, b = (st_.piece + q // BLOCKS) % RING, q % BLOCKS
                hi = w_hi[:, slot, b * P:(b + 1) * P]
                lo = w_lo[:, slot, b * P:(b + 1) * P]
                if norm is not None:
                    pe.wait_ge(norm.ready, c + 1)
                if ready is not None:
                    pe.wait_ge(ready, c + 1)
                a = rhs(c)

                def high():
                    return nc.tensor.matmul(bank[:, :], hi, a, start=c == 0, stop=c == chunks - 1,
                                            skip_group_check=True)

                def cross():
                    return nc.tensor.matmul(bank[:, T:2 * T], lo, a[:, 0:T], start=False, stop=False,
                                            skip_group_check=True)
                if c == 0:
                    high()
                    last = cross()
                else:
                    cross()
                    last = high()
                if q % BLOCKS == BLOCKS - 1:
                    last.then_inc(piece_used, 1)
                elif c == chunks - 1 and tile_sem is not None:
                    last.then_inc(tile_sem, 1)
                if norm is not None and norm.by_tensor:
                    pe.wait_ge(norm.squared, c + 1)
                    nc.tensor.matmul(psN[:, 0:T], ones[:, :], four_squares(c), start=c == 0,
                                     stop=c == chunks - 1, skip_group_check=True).then_inc(norm.added, 1)

        def scalar_split(act, stage, dp, k, ahead=RING):
            n = STAGES[stage].piece + k
            if ahead:
                act.wait_ge(piece_used, dp + (n + 1))
            m = n + ahead
            act.wait_ge(landed[m % RING], dp * (16 // RING) + 16 * (m // RING + 1))
            nc.scalar.activation(w_hi[:, m % RING, :], raw[:, m % RING, :], ACT.Copy).then_inc(hi_ready, 1)

        def vector_split(dve, stage, dp, k, ahead=RING):
            m = STAGES[stage].piece + k + ahead
            dve.wait_ge(hi_ready, dp + (m + 1))
            s = m % RING
            nc.vector.tensor_tensor(w_lo[:, s, :], raw[:, s, :], w_hi[:, s, :].bitcast(F32),
                                    ALU.subtract).then_inc(split_done, 1)

        def scalar_low(act, stage, dp, k, tile):
            act.wait_ge(piece_used, dp + (STAGES[stage].piece + k + 1))
            b = (STAGES[stage].tile + tile) % 2
            nc.scalar.activation(low[:, b, :], ps[b][:, T:2 * T], ACT.Copy).then_inc(low_copied, 1)

        def vector_sum(dve, stage, dt, tile, dst):
            n = STAGES[stage].tile + tile
            dve.wait_ge(low_copied, dt + (n + 1))
            nc.vector.tensor_tensor(dst, low[:, n % 2, :], ps[n % 2][:, 0:T], ALU.add)\
                .then_inc(tile_summed, 1)

        def summed(stage, dt, tile):
            return dt + (STAGES[stage].tile + tile + 3)

        class Norm:

            def __init__(self, name, by_tensor=False):
                self.by_tensor = by_tensor
                self.squared = sem(f"{name}_squared")
                self.added = sem(f"{name}_added")
                self.sums = sem(f"{name}_sums")
                self.root = sem(f"{name}_root")
                self.rstd = sem(f"{name}_rstd")
                self.high = sem(f"{name}_high")
                self.ready = sem(f"{name}_ready")

        norms = {name: Norm(name, name in ("mlp2", "ple2"))
                 for name in ("mix1", "ffn1", "final", "mix2", "mixed2", "mlp2", "mlped2", "ple2", "pled2")}

        def square_free(act, n, i, b):
            act.wait_ge(n.added, i * 2 + (b + 1))

        def square(act, n, b, src, scale=1.0, buf=None):
            buf = sq2 if buf is None else buf
            nc.scalar.activation(buf[:, b, :], src, ACT.Square, scale=scale).then_inc(n.squared, 1)

        def add_squares(pool, n):
            nc.gpsimd.memset(total[:, :], 0.0).then_inc(n.added, 2)
            pool.wait_ge(n.added, 2)
            with nc.gpsimd.Fori(0, KD // 2 - 1) as i:
                for b in range(2):
                    pool.wait_ge(n.squared, i * 2 + (b + 1))
                    pool.wait_ge(n.added, i * 2 + (b + 2))
                    nc.gpsimd.tensor_tensor(total[:, :], total[:, :], sq2[:, b, :], ALU.add).then_inc(n.added, 1)
            pool.wait_ge(n.squared, KD - 1)
            pool.wait_ge(n.added, KD)
            nc.gpsimd.tensor_tensor(total[:, :], total[:, :], sq2[:, 0, :], ALU.add).then_inc(n.added, 1)

        def norm_tensor(pe, n):
            pe.wait_ge(n.added, KD + 1)
            nc.tensor.matmul(psN[:, 0:T], ones[:, :], total[:, :], start=True, stop=False)
            pe.wait_ge(n.squared, KD)
            nc.tensor.matmul(psN[:, 0:T], ones[:, :], sq2[:, 1, :], start=False, stop=True).then_inc(n.sums, 1)

        def total_tensor(pe, n, src, half):
            pe.wait_ge(n.added, KD + 2)
            nc.tensor.matmul(psN[:, half * T:(half + 1) * T], ones[:, :], src[:, :], start=True, stop=True)\
                .then_inc(n.sums, 1)

        def norm_root(act, n):
            if n.by_tensor:
                act.wait_ge(n.added, KD)
            else:
                act.wait_ge(n.sums, 1)
            nc.scalar.activation(root[:, :], psN[:, 0:T], ACT.Sqrt, bias=eps[:, 0:1], scale=1.0 / D)\
                .then_inc(n.root, 1)

        def norm_rstd(dve, n, dst=None):
            dve.wait_ge(n.root, 1)
            nc.vector.reciprocal((rstd if dst is None else dst)[:, :], root[:, :]).then_inc(n.rstd, 1)

        def h_high(act, n, c, g):
            nc.scalar.activation(h[:, c, 0:T], x[:, c, :], ACT.Copy, scale=g).then_inc(n.high, 1)

        def h_low(dve, n, i, b, g):
            c = i * 2 + b
            dve.wait_ge(n.high, i * 2 + (b + 1))
            nc.vector.scalar_tensor_tensor(out=h[:, c, T:2 * T], in0=x[:, c, :], scalar=g,
                                           in1=h[:, c, 0:T].bitcast(F32), op0=ALU.mult, op1=ALU.subtract)\
                .then_inc(n.ready, 1)

        def vector_scale(dve, stage, dt, tile, dst, src):
            dve.wait_ge(tile_summed, summed(stage, dt, tile))
            nc.vector.tensor_tensor(dst, src, rstd[:, :], ALU.mult).then_inc(tile_scaled, 1)

        def scaled(stage, before, tile):
            return before + (STAGES[stage].scaled + tile + 1)

        def h_chunk(c):
            return h[:, c, :]

        def merged_chunk(c):
            return merged_hl[:, c, :]

        def y_chunk(c):
            return y[:, c, :]

        rnn_v = S("conv0 conv1 conv2 u inner gap hid y low", "rnn_vector")
        rnn_a = S("r i gelu_sig a th sqrt high", "rnn_scalar")
        rnn_p = S("gates", "rnn_tensor")
        rnn_g = S("y2 y3 iu gl a2 b_in", "rnn_gpsimd")
        wgate_landed = sem("wgate_landed")
        decay_log = sem("decay_log_sigmoid")
        even_added = sem("even_squares_added")
        odd_added = sem("odd_squares_added")
        forget_log = sem("forget_log_sigmoid")
        branch_mul = {s: sem(f"{s}_gated") for s in ("rnn_branch", "attn_branch", "pool_branch")}
        gates_done = {s: sem(f"{s}_gate_sigmoid") for s in ("rnn", "attn", "pool")}
        forget_p = S("FT", "forget_tensor")
        att_v = S("fsel s max nmax recip p0 p1 vtok low", "attn_vector")
        att_a = S("bias0 bias1 e0 e1 prT high", "attn_scalar")
        att_p = S("scores fk vT pT out", "attn_tensor")
        att_g = S("biasm", "attn_gpsimd")
        pooled_done = sem("pooled_done")
        poolx_pad = sem("poolx_pad")
        pool_p = S("y0 y1 y2 y3", "pool_tensor")
        pool_a = S(" ".join(f"s{c} h{c}" for c in range(8)), "pool_scalar")
        pool_v = S(" ".join(f"l{c}" for c in range(8)), "pool_vector")
        merged_added = sem("merged_added")
        merged_high = sem("merged_high")
        merged_low = sem("merged_low")
        const2_landed = sem("const2_landed")
        const3_landed = sem("const3_landed")
        const4_landed = sem("const4_landed")
        x_added = sem("x_added")
        up_v = S("prod low", "up_vector")
        up_a = S("silu high", "up_scalar")
        down_x = sem("down_x_added")

        kv_v = S("g rstd cos sin sum k vtok", "kv_vector")
        kv_a = S("square root", "kv_scalar")
        kv_p = S("stat turn v", "kv_tensor")
        b2_v = S("g rstd cos sin sum q maxA nmaxA recipA p0A p1A sB maxB nmaxB recipB p0B p1B lowA",
                 "heads_vector")
        b2_a = S("square root e0A e1A pAT e0B e1B highA", "heads_scalar")
        b2_p = S("stat turn scoresA scoresB pTA outA", "heads_tensor")
        tail_v = S("vtok low", "tail_vector")
        tail_a = S("pT high", "tail_scalar")
        tail_p = S("pT vT out", "tail_tensor")
        b2_g = S("rbm", "heads_gpsimd")
        rbias_landed = sem("rbias_landed")
        sq_v = S("sq low", "mlp_vector")
        sq_a = S("high", "mlp_scalar")
        acc_zero = sem("acc_zeroed")
        acc_added = sem("acc_added")
        p_split = sem("p_split")
        ple_a = sem("ple_sigmoid")
        ple_v = sem("ple_gated")
        stored = sem("stored")
        x_landed = [sem(f"x_landed{n}") for n in range(4)]
        x_mixed = sem("x_mixed")
        x_mlped = sem("x_mlped")
        x_final = sem("x_final")
        post_gained = sem("post_gained")
        result_t = sem("result_scaled")
        result_v = sem("result_by_vector")
        result_g = sem("result_by_gpsimd")
        p_landed = sem("p_landed")

        block = ctx.enter_context(nc.Block())

        @block.sync
        def _(sp):
            def load(n, group):
                sp.dma_start(raw[:, n % RING, :], w[group, n % RING]).then_inc(landed[n % RING], 16)

            def load_x(n):
                c = slice(4 * n, 4 * n + 4)
                sp.dma_start(x[:, c, :], xT[:, c, :]).then_inc(x_landed[n], 16)

            sp.dma_start(cols[:, :], columns).then_inc(columns_landed, 16)
            load(0, 0)
            load_x(0)
            load_x(1)
            load_x(2)
            load(1, 0)
            load_x(3)
            load(2, 0)
            load(3, 0)
            sp.dma_start(ident[:, :], unit).then_inc(unit_landed, 16)
            with nc.sync.Fori(1, PIECES // RING) as g:
                for r in range(RING):
                    sp.wait_ge(split_done, g * RING + (r + 1 - RING))
                    load(r, g)
            for r in range(PIECES % RING):
                n = PIECES // RING * RING + r
                sp.wait_ge(split_done, n + 1 - RING)
                load(r, PIECES // RING)
            for first in range(0, KD, 2):
                c = slice(first, first + 2)
                sp.wait_ge(result_v, min(first + 2, RESULT_V))
                if first + 2 > RESULT_V:
                    sp.wait_ge(result_g, 2 * (first + 2 - RESULT_V))
                sp.dma_start(outT[:, c, :], x[:, c, :]).then_inc(stored, 16)
            sp.wait_ge(stored, KD // 2 * 16)

        @block.gpsimd
        def _(pool):

            def mul(dst, a, b, after, done):
                for s_, v in after:
                    pool.wait_ge(s_, v)
                nc.gpsimd.tensor_tensor(dst, a, b, ALU.mult).then_inc(*done)

            def log_sigmoid(buf, x_, factor, dst, done):
                B = lambda k: buf[:, k, :]
                count = [0]

                def step(ins):
                    count[0] += 1
                    ins.then_inc(done, 1)
                    pool.wait_ge(done, count[0])

                step(nc.gpsimd.tensor_tensor(B(5), B(4), B(4), ALU.mult))
                step(nc.gpsimd.tensor_scalar(B(6), B(5), 1.0 / 19.0, None, ALU.mult))
                for odd in (17, 15, 13, 11, 9, 7, 5, 3):
                    step(nc.gpsimd.tensor_scalar(B(6), B(6), 1.0 / odd, None, ALU.add))
                    step(nc.gpsimd.tensor_tensor(B(6), B(6), B(5), ALU.mult))
                step(nc.gpsimd.tensor_scalar(B(6), B(6), 1.0, -2.0 * factor, ALU.add, ALU.mult))
                step(nc.gpsimd.tensor_tensor(B(6), B(6), B(4), ALU.mult))
                step(nc.gpsimd.tensor_scalar(B(1), x_, 0.0, factor, ALU.min, ALU.mult))
                step(nc.gpsimd.tensor_tensor(dst, B(6), B(1), ALU.add))
                assert count[0] == LOG_SIGMOID_STEPS

            pool.wait_ge(vector_chain, LS_STEPS)
            log_sigmoid(ls, cols[:, COL["lam"]:COL["lam"] + 8], 8.0, decay[:, :], decay_log)
            nc.gpsimd.memset(total[:, :], 0.0).then_inc(even_added, 1)
            for k in range(KD // 2):
                pool.wait_ge(norms["mix1"].squared, 2 * k + 1)
                pool.wait_ge(even_added, k + 1)
                nc.gpsimd.tensor_tensor(total[:, :], total[:, :], four_squares(2 * k), ALU.add)\
                    .then_inc(even_added, 1)
            with nc.gpsimd.Fori(0, 8) as i:
                pool.dma_start(wgate[:, :], w_gates[i]).then_inc(wgate_landed, 16)
                mul(y2[:, :], ry[:, :], ry[:, :], [(tile_scaled, scaled("rnn", i * 4, 1))], rnn_g.done("y2"))
                mul(y3[:, :], y2[:, :], ry[:, :], [(rnn_g.sem, rnn_g.at("y2", i))], rnn_g.done("y3"))
                mul(iu[:, :], i_g[:, :], u[:, :], [(rnn_a.sem, rnn_a.at("i", i))], rnn_g.done("iu"))
                mul(gl[:, :], ry[:, :], sg[:, :], [(rnn_a.sem, rnn_a.at("gelu_sig", i))], rnn_g.done("gl"))
                mul(a2[:, :], a_t[:, :], a_t[:, :], [(rnn_a.sem, rnn_a.at("a", i))], rnn_g.done("a2"))
                mul(b_in[:, :], sq[:, :], iu[:, :], [(rnn_a.sem, rnn_a.at("sqrt", i)), (rnn_g.sem, rnn_g.at("iu", i))],
                    rnn_g.done("b_in"))
            pool.wait_ge(vector_chain, F_STEPS - 2)
            log_sigmoid(lf, lf[:, 0, :], 1.0, lf[:, 7, :], forget_log)
            pool.wait_ge(rnn_v.sem, rnn_v.at("low", 7))
            pool.dma_start(cmask[:, :, :], causal_mask).then_inc(const2_landed, 16)
            pool.wait_ge(const2_landed, 16)
            with nc.gpsimd.Fori(0, 8) as i:
                pool.wait_ge(att_a.sem, att_a.at("bias1", i))
                nc.gpsimd.tensor_tensor(biasm[:, :, :], bias[:, :, :], cmask[:, :, :], ALU.add)\
                    .then_inc(*att_g.done("biasm"))
            pool.wait_ge(att_v.sem, att_v.at("low", 7))
            pool.dma_start(inv[:, :, :], inv_count).then_inc(const3_landed, 16)
            pool.dma_start(wpool[:, :, :, :], w_pool).then_inc(const3_landed, 16)
            pool_steps = [0]

            def step(ins):
                pool_steps[0] += 1
                ins.then_inc(pooled_done, 1)
                pool.wait_ge(pooled_done, pool_steps[0])

            step(nc.gpsimd.memset(sums[:, :, :, :], 0.0))
            pool.wait_ge(poolx_pad, 1)
            pool.wait_ge(const3_landed, 32)
            for g in range(4):
                src = pool_x[:, 2 * g:2 * g + 2, :]
                for level in range(g + 1):
                    lag = 1 << level
                    dst = sums[:, level % 2, :, :]
                    step(nc.gpsimd.tensor_tensor(dst[:, :, 16:PADT], src[:, :, 16:PADT],
                                                 src[:, :, 16 - lag:PADT - lag], ALU.add))
                    src = dst
                means = sums[:, (g + 1) % 2, :, 16:PADT]
                for m in range(2):
                    step(nc.gpsimd.tensor_tensor(means[:, m, :], src[:, m, 16:PADT], inv[:, g, :], ALU.mult))
                step(nc.gpsimd.tensor_tensor(pooled[:, 2 * g:2 * g + 2, :], means,
                                             pool_x[:, 2 * g:2 * g + 2, 16:PADT], ALU.subtract))
            for o in range(KD):
                pool.wait_ge(branch_mul["pool_branch"], o + 1)
                nc.gpsimd.tensor_tensor(merged[:, o, :], merged[:, o, :], tmp[:, o % 2, :], ALU.add)\
                    .then_inc(merged_added, 1)
            add_squares(pool, norms["ffn1"])
            pool.wait_ge(norms["ffn1"].sums, 1)
            a, b_ = norms["final"], norms["mix2"]
            nc.gpsimd.memset(total[:, :], 0.0).then_inc(a.added, 2)
            nc.gpsimd.memset(total_g[:, :], 0.0).then_inc(b_.added, 2)
            with nc.gpsimd.Fori(0, 8) as i:
                for b in range(2):
                    for n, buf, into in ((a, sq2, total), (b_, sqg2, total_g)):
                        pool.wait_ge(n.squared, i * 2 + (b + 1))
                        pool.wait_ge(n.added, i * 2 + (b + 2))
                        nc.gpsimd.tensor_tensor(into[:, :], into[:, :], buf[:, b, :], ALU.add).then_inc(n.added, 1)
            pool.wait_ge(down_x, 16)
            for dst, src in ((cos_t[:, :], rope_cos), (sin_t[:, :], rope_sin), (turn[:, :], rope_turn),
                             (nmask[:, :, :], near_mask)):
                pool.dma_start(dst, src).then_inc(const4_landed, 16)
            pool.wait_ge(const4_landed, 64)
            with nc.gpsimd.Fori(0, 8) as i:
                pool.wait_ge(rbias_landed, i * 16 + 16)
                nc.gpsimd.tensor_tensor(rbm[:, :, :], rbias[:, :, :], nmask[:, :, :], ALU.add)\
                    .then_inc(*b2_g.done("rbm"))
            pool.wait_ge(tail_v.sem, tail_v.at("low", 7))
            pool.dma_start(p_raw[:, :, :], pT).then_inc(p_landed, 16)

            def update(n, src, gained):
                pool.wait_ge(n.rstd, 1)
                pool.wait_ge(gained, KD)
                for c in range(KD):
                    nc.gpsimd.tensor_tensor(src[:, c, :], src[:, c, :], rstd_x[:, :], ALU.mult)\
                        .then_inc(post_scaled, 1)

            pool.wait_ge(norms["mix2"].sums, 1)
            add_squares(pool, norms["mixed2"])
            update(norms["mixed2"], mix32, mix_gained)
            pool.wait_ge(x_mixed, 16)
            nc.gpsimd.memset(acc[:, :, :], 0.0).then_inc(acc_zero, 1)
            add_squares(pool, norms["mlped2"])
            update(norms["mlped2"], acc, post_gained)
            add_squares(pool, norms["pled2"])
            pool.wait_ge(norms["pled2"].rstd, 1)
            pool.wait_ge(e_gained, KD)
            for k, c in enumerate(range(RESULT_V, KD)):
                nc.gpsimd.tensor_tensor(e[:, c, :], e[:, c, :], rstd_x[:, :], ALU.mult).then_inc(result_g, 1)
                pool.wait_ge(result_g, 2 * k + 1)
                nc.gpsimd.tensor_tensor(x[:, c, :], x[:, c, :], e[:, c, :], ALU.add).then_inc(result_g, 1)

        POOLED = [1 + sum(k + 1 + 3 for k in range(g + 1)) for g in range(4)]

        @block.scalar
        def _(act):
            def split(stage, dp, k):
                scalar_split(act, stage, dp, k)

            def act_op(dst, src, fn, after, done, **kw):
                for s_, v in after:
                    act.wait_ge(s_, v)
                return nc.scalar.activation(dst, src, fn, **kw).then_inc(*done)

            act_op(ls[:, 3, :], ls[:, 2, :], ACT.Exp, [(vector_chain, LS_STEPS - 3)], (scalar_chain, 1),
                   scale=-1.0)
            scalar_split(act, "rnn", 0, 0, ahead=0)
            act.wait_ge(columns_landed, 16)
            for k in range(4):
                act.wait_ge(x_landed[k], 16)
                for c in range(4 * k, 4 * k + 4):
                    h_high(act, norms["mix1"], c, col("g_mix", c))
                if k > 1:
                    scalar_split(act, "rnn", 0, k - 1, ahead=0)
            for c in range(KD):
                if c >= 4:
                    act.wait_ge((even_added, odd_added)[c % 2], c // 2)
                nc.scalar.activation(four_squares(c), x[:, c, :], ACT.Square).then_inc(norms["mix1"].squared, 1)
                if c == 3:
                    scalar_split(act, "rnn", 0, 3, ahead=0)

            act.wait_ge(decay_log, LOG_SIGMOID_STEPS)
            def recurrence(i, first):
                dp, dt = i * 8, i * 4
                split("rnn", dp, 0)
                scalar_low(act, "rnn", dp, 1, 0)
                split("rnn", dp, 1)
                if first:
                    act.wait_ge(vector_chain, 3)
                    norm_root(act, norms["mix1"])
                split("rnn", dp, 2)
                scalar_low(act, "rnn", dp, 3, 1)
                split("rnn", dp, 3)
                split("rnn", dp, 4)
                act_op(r_g[:, :], psS[:, 0, :], ACT.Sigmoid, [(rnn_p.sem, rnn_p.at("gates", i))],
                       rnn_a.done("r"), bias=col("b_rg", i))
                act_op(i_g[:, :], psS[:, 1, :], ACT.Sigmoid, [], rnn_a.done("i"), bias=col("b_ig", i))
                act_op(sg[:, :], inner[:, :], ACT.Sigmoid, [(rnn_v.sem, rnn_v.at("inner", i))],
                       rnn_a.done("gelu_sig"), scale=2.0 * math.sqrt(2.0 / math.pi))
                act_op(a_t[:, :], r_g[:, :], ACT.Exp, [(rnn_a.sem, rnn_a.at("r", i))], rnn_a.done("a"),
                       scale=decay[:, ds(i, 1)])
                act_op(th[:, :], r_g[:, :], ACT.Tanh, [], rnn_a.done("th"), scale=decay[:, ds(i, 1)])
                scalar_low(act, "rnn", dp, 5, 2)
                split("rnn", dp, 5)
                split("rnn", dp, 6)
                act_op(sq[:, :], gap[:, :], ACT.Sqrt, [(rnn_v.sem, rnn_v.at("gap", i))], rnn_a.done("sqrt"),
                       scale=-1.0)
                scalar_low(act, "rnn", dp, 7, 3)
                split("rnn", dp, 7)
                for b in range(2):
                    act_op(gate[:, i * 2 + b, :], tsum[:, b, :], ACT.Sigmoid,
                           [(tile_scaled, scaled("rnn", dt, 2 + b))], (gates_done["rnn"], 1))
                act_op(y[:, i, 0:T], y_r[:, :], ACT.Copy, [(rnn_v.sem, rnn_v.at("y", i))], rnn_a.done("high"))

            recurrence(0, True)
            with nc.scalar.Fori(1, 8) as i:
                recurrence(i, False)

            split("forget", 0, 0)
            scalar_low(act, "forget", 0, 1, 0)
            split("forget", 0, 1)
            act_op(lf[:, 3, :], lf[:, 2, :], ACT.Exp, [(vector_chain, LS_STEPS + 3)],
                   (scalar_chain, 1), scale=-1.0)

            def branch(stage):
                with nc.scalar.Fori(0, 4) as i:
                    for t in range(4):
                        scalar_low(act, stage, i * 4, t, t)
                        split(stage, i * 4, t)
                        if stage == "pool_branch":
                            o = i * 4 + t
                            act.wait_ge(merged_added, i * 4 + (t + 1))
                            nc.scalar.activation(merged_hl[:, o, 0:T], merged[:, o, :], ACT.Copy)\
                                .then_inc(merged_high, 1)

            branch("rnn_branch")

            with nc.scalar.Fori(0, 8) as i:
                dp, dt = i * 12, i * 6
                for k in range(6):
                    if k % 2:
                        scalar_low(act, "attn", dp, k, k // 2)
                    split("attn", dp, k)
                split("attn", dp, 6)
                for b in range(2):
                    act_op(bias[:, b, :], psF[:, 0, :], ACT.Identity, [(att_p.sem, att_p.at("fk", i))],
                           att_a.done(f"bias{b}"), scale=-1.0, bias=f_t[:, b, ds(i, 1)])
                scalar_low(act, "attn", dp, 7, 3)
                split("attn", dp, 7)
                for b in range(2):
                    act_op(pr[:, b, :], sc[:, b, :], ACT.Exp, [(att_v.sem, att_v.at("nmax", i))],
                           att_a.done(f"e{b}"), bias=st[:, 2 + b:3 + b], accum_out=st[:, 4 + b:5 + b])
                split("attn", dp, 8)
                scalar_low(act, "attn", dp, 9, 4)
                split("attn", dp, 9)
                split("attn", dp, 10)
                act_op(prT[:, :, :], psT[:, :, :], ACT.Copy, [(att_p.sem, att_p.at("pT", i))], att_a.done("prT"))
                scalar_low(act, "attn", dp, 11, 5)
                split("attn", dp, 11)
                for b in range(2):
                    act_op(gate[:, i * 2 + b, :], tsum[:, b, :], ACT.Sigmoid,
                           [(tile_scaled, scaled("attn", dt, 4 + b))], (gates_done["attn"], 1))
                act_op(y[:, i, 0:T], psO[:, 0:T], ACT.Copy, [(att_p.sem, att_p.at("out", i))], att_a.done("high"))
            branch("attn_branch")

            def pool_gates(i):
                for b in range(2):
                    split("pool", i * 4, 2 * b)
                    scalar_low(act, "pool", i * 4, 2 * b + 1, b)
                    split("pool", i * 4, 2 * b + 1)
                    act_op(gate[:, i * 2 + b, :], tsum[:, b, :], ACT.Sigmoid,
                           [(tile_scaled, scaled("pool", i * 2, b))], (gates_done["pool"], 1))

            with nc.scalar.Fori(0, POOLED_AFTER) as i:
                pool_gates(i)
            for c in range(8):
                g, m = c // 2, c % 2
                bank = (psS, psF, psT)[g % 3]
                act_op(tmp[:, m, :], bank[:, m, :], ACT.Identity, [(pool_p.sem, pool_p.at(f"y{g}"))]
                       + ([(pool_v.sem, pool_v.at(f"l{c - 2}"))] if c >= 2 else []),
                       pool_a.done(f"s{c}"), scale=col("pool_scale", c))
                act_op(y[:, c, 0:T], tmp[:, m, :], ACT.Copy, [(pool_a.sem, pool_a.at(f"s{c}"))],
                       pool_a.done(f"h{c}"))
            with nc.scalar.Fori(POOLED_AFTER, 8) as i:
                pool_gates(i)
            branch("pool_branch")

            def plain(stage, tiles, per_tile, body=2):
                with nc.scalar.Fori(0, tiles // body) as i:
                    for t in range(body):
                        for k in range(per_tile):
                            if k == per_tile - 1:
                                scalar_low(act, stage, i * (body * per_tile), t * per_tile + k, t)
                            split(stage, i * (body * per_tile), t * per_tile + k)

            with nc.scalar.Fori(0, 8) as i:
                for b in range(2):
                    split("out", i * 4, 2 * b)
                    scalar_low(act, "out", i * 4, 2 * b + 1, b)
                    split("out", i * 4, 2 * b + 1)
                    square_free(act, norms["ffn1"], i, b)
                    act.wait_ge(x_added, i * 2 + (b + 1))
                    h_high(act, norms["ffn1"], i * 2 + b, col("g_ffn", i * 2 + b))
                    square(act, norms["ffn1"], b, x[:, i * 2 + b, :])
            norm_root(act, norms["ffn1"])
            with nc.scalar.Fori(0, KF) as i:
                dp, dt = i * 4, i * 2
                split("up", dp, 0)
                scalar_low(act, "up", dp, 1, 0)
                split("up", dp, 1)
                act_op(tmp[:, 1, :], tsum[:, 0, :], ACT.Silu, [(tile_scaled, scaled("up", dt, 0))],
                       up_a.done("silu"))
                split("up", dp, 2)
                scalar_low(act, "up", dp, 3, 1)
                split("up", dp, 3)
                act_op(hidden[:, i, 0:T], tmp[:, 0, :], ACT.Copy, [(up_v.sem, up_v.at("prod", i))],
                       up_a.done("high"))
            act.wait_ge(g_both_ready, 1)
            with nc.scalar.Fori(0, 2) as i:
                for k in range(KF):
                    for t in DOWN_ENDS.get(k, []):
                        scalar_low(act, "down", i * KF, k, t)
                    split("down", i * KF, k)
                    for t in DOWN_ENDS.get(k, []):
                        c = i * 8 + t
                        square_free(act, norms["final"], i * 4 + t // 2, t % 2)
                        square_free(act, norms["mix2"], i * 4 + t // 2, t % 2)
                        act.wait_ge(down_x, i * 8 + (t + 1))
                        h_high(act, norms["mix2"], c, g_both[:, ds(c, 1)])
                        square(act, norms["final"], t % 2, x[:, c, :])
                        square(act, norms["mix2"], t % 2, x[:, c, :], col("g_final", c), sqg2)
            act.wait_ge(squared_mix, 2)
            nc.scalar.activation(root[:, :], tmp[:, 1, :], ACT.Sqrt).then_inc(norms["mix2"].root, 1)
            nc.scalar.activation(tmp[:, 0, :], psN[:, 0:T], ACT.Sqrt, bias=eps[:, 0:1], scale=1.0 / D)\
                .then_inc(norms["final"].root, 1)

            act.wait_ge(down_x, 16)
            def heads(m, dp, dt, tail):
                act.dma_start(rbias[:, :, :], rel_bias[m]).then_inc(rbias_landed, 16)
                if tail:
                    act_op(pBT[:, :, :], psS[:, :, :], ACT.Copy, [(tail_p.sem, tail_p.at("pT", m - 1))],
                           tail_a.done("pT"))
                split("mix", dp, 4)
                scalar_low(act, "mix", dp, 5, 2)
                split("mix", dp, 5)
                act_op(rsq[:, :], rv[:, :], ACT.Square, [(tile_scaled, scaled("mix", dt, 2))],
                       b2_a.done("square"))
                if tail:
                    tail_high(m - 1)
                split("mix", dp, 6)
                act_op(root[:, :], psN[:, 0:T], ACT.Sqrt, [(b2_p.sem, b2_p.at("turn", m))],
                       b2_a.done("root"), bias=eps[:, 0:1], scale=1.0 / P)
                scalar_low(act, "mix", dp, 7, 3)
                split("mix", dp, 7)
                split("mix", dp, 8)
                for b in range(2):
                    act_op(pA[:, b, :], psS[:, b, :], ACT.Exp, [(b2_v.sem, b2_v.at("nmaxA", m))],
                           b2_a.done(f"e{b}A"), scale=SCALE, bias=stA[:, 2 + b:3 + b],
                           accum_out=stA[:, 4 + b:5 + b])
                scalar_low(act, "mix", dp, 9, 4)
                split("mix", dp, 9)
                act_op(pAT[:, :, :], psT[:, :, :], ACT.Copy, [(b2_p.sem, b2_p.at("pTA", m))],
                       b2_a.done("pAT"))
                for b in range(2):
                    act_op(pB[:, b, :], sB[:, b, :], ACT.Exp, [(b2_v.sem, b2_v.at("nmaxB", m))],
                           b2_a.done(f"e{b}B"), bias=stB[:, 2 + b:3 + b], accum_out=stB[:, 4 + b:5 + b])
                split("mix", dp, 10)
                scalar_low(act, "mix", dp, 11, 5)
                act_op(mixed[:, m, 0:T], psO[:, 0:T], ACT.Copy, [(b2_p.sem, b2_p.at("outA", m))],
                       b2_a.done("highA"))
                split("mix", dp, 11)

            def tail_high(m):
                act_op(mixed[:, m + 8, 0:T], psO[:, T:2 * T], ACT.Copy, [(tail_p.sem, tail_p.at("out", m))],
                       tail_a.done("high"))

            for j in range(2):
                dp = j * 36
                split("mix", dp, 0)
                scalar_low(act, "mix", dp, 1, 0)
                split("mix", dp, 1)
                act_op(rsq[:, :], rv[:, :], ACT.Square, [(tile_scaled, scaled("mix", j * 18, 0))],
                       kv_a.done("square"))
                split("mix", dp, 2)
                scalar_low(act, "mix", dp, 3, 1)
                split("mix", dp, 3)
                act_op(root[:, :], psN[:, 0:T], ACT.Sqrt, [(kv_p.sem, kv_p.at("turn", j))], kv_a.done("root"),
                       bias=eps[:, 0:1], scale=1.0 / P)
                if j == 0:
                    heads(0, 0, 0, False)
                with nc.scalar.Fori(1 - j, 4) as i:
                    heads(i + j * 4, i * 8 + j * 36, i * 4 + j * 18, True)
            act_op(pBT[:, :, :], psS[:, :, :], ACT.Copy, [(tail_p.sem, tail_p.at("pT", 7))], tail_a.done("pT"))
            tail_high(7)
            with nc.scalar.Fori(0, 8) as i:
                for b in range(2):
                    split("wo", i * 4, 2 * b)
                    scalar_low(act, "wo", i * 4, 2 * b + 1, b)
                    split("wo", i * 4, 2 * b + 1)
                    square_free(act, norms["mixed2"], i, b)
                    act.wait_ge(tile_summed, summed("wo", i * 2, b))
                    square(act, norms["mixed2"], b, tsum[:, b, :])
                    nc.scalar.activation(mix32[:, i * 2 + b, :], tsum[:, b, :], ACT.Copy,
                                         scale=col("post_mix", i * 2 + b)).then_inc(mix_gained, 1)

            def updated(n, before, added):
                gains = "pre_mlp" if n is norms["mlp2"] else "pre_ple"
                early = 0 if n is norms["mlp2"] else EARLY
                if not early:
                    norm_root(act, before)
                for c in range(KD):
                    if c >= early:
                        act.wait_ge(added, c + 1)
                        h_high(act, n, c, col(gains, c))
                    if c >= 4:
                        act.wait_ge(n.added, c - 3)
                    nc.scalar.activation(four_squares(c), x[:, c, :], ACT.Square).then_inc(n.squared, 1)
                norm_root(act, n)

            updated(norms["mlp2"], norms["mixed2"], x_mixed)

            for j in range(2):
                if j == 1:
                    act_op(p_hl[:, :, 0:T], p_raw[:, :, :], ACT.Copy, [(p_landed, 16)], (p_split, 1))
                with nc.scalar.Fori(0, 16) as i:
                    dp = j * 128 + i * 4
                    for b in range(2):
                        split("mlp", dp, 2 * b)
                        scalar_low(act, "mlp", dp, 2 * b + 1, b)
                        split("mlp", dp, 2 * b + 1)
                        act_op(hidden2[:, i * 2 + b, 0:T], tmp[:, b, :], ACT.Copy,
                               [(sq_v.sem, sq_v.at("sq", j * 32 + i * 2 + b))], sq_a.done("high"))
                with nc.scalar.Fori(0, 8) as i:
                    dp = j * 128 + i * 8
                    for k in range(8):
                        if k % 4 == 3:
                            scalar_low(act, "mlp", dp, 64 + k, k // 4)
                        split("mlp", dp, 64 + k)
                        if k % 4 == 3 and j == 1:
                            b = k // 4
                            square_free(act, norms["mlped2"], i, b)
                            act.wait_ge(acc_added, i * 2 + (KD + b + 1))
                            square(act, norms["mlped2"], b, acc[:, i * 2 + b, :])
                            nc.scalar.activation(acc[:, i * 2 + b, :], acc[:, i * 2 + b, :], ACT.Copy,
                                                 scale=col("post_mlp", i * 2 + b)).then_inc(post_gained, 1)

            def early_high(c):
                act.wait_ge(x_mlped, c + 1)
                h_high(act, norms["ple2"], c, col("pre_ple", c))

            for t in range(16):
                k = t // 4
                if t % 4 < 3:
                    act.wait_ge(ple_tile_done, 3 * k + t % 4 + 1)
                    b = (STAGES["ple"].tile + t) % 2
                    nc.scalar.activation(low[:, b, :], ps[b][:, T:2 * T], ACT.Copy).then_inc(low_copied, 1)
                else:
                    scalar_low(act, "ple", 0, k, t)
                    split("ple", 0, k)
                if t == 5:
                    norm_root(act, norms["mlped2"])
                if t > KD - EARLY:
                    early_high(t - (KD - EARLY) - 1)
            early_high(EARLY - 1)
            updated(norms["ple2"], norms["mlped2"], x_mlped)

            def embed(i, last):
                def gate_(b):
                    act_op(tmp[:, b, :], tsum[:, b, :], ACT.Sigmoid,
                           [(tile_scaled, scaled("ple_gate", i * 2, b))], (ple_a, 1))

                def gated(b):
                    square_free(act, norms["pled2"], i, b)
                    act.wait_ge(ple_v, i * 2 + (b + 1))
                    c = i * 2 + b
                    square(act, norms["pled2"], b, e[:, c, :])
                    nc.scalar.activation(e[:, c, :], e[:, c, :], ACT.Copy, scale=col("post_ple", c))\
                        .then_inc(e_gained, 1)

                def split_(k):
                    if not last:
                        split("ple_gate", i * 4, k)

                split_(0)
                scalar_low(act, "ple_gate", i * 4, 1, 0)
                split_(1)
                gate_(0)
                split_(2)
                gated(0)
                scalar_low(act, "ple_gate", i * 4, 3, 1)
                split_(3)
                gate_(1)
                gated(1)

            with nc.scalar.Fori(0, 7) as i:
                embed(i, False)
            embed(7, True)
            norm_root(act, norms["pled2"])

        @block.vector
        def _(dve):
            chain = [0]

            def link(ins):
                chain[0] += 1
                ins.then_inc(vector_chain, 1)
                dve.wait_ge(vector_chain, chain[0])

            def split(stage, dp, k):
                vector_split(dve, stage, dp, k)

            def vsum(stage, dt, tile, dst):
                vector_sum(dve, stage, dt, tile, dst)

            def vscaled(stage, dt, tile, sums, dst=None):
                vsum(stage, dt, tile, sums)
                vector_scale(dve, stage, dt, tile, sums if dst is None else dst, sums)

            def tt(dst, a, b, op, after, done):
                for s_, v in after:
                    dve.wait_ge(s_, v)
                nc.vector.tensor_tensor(dst, a, b, op).then_inc(*done)

            def ts(dst, a, s1, s2, op0, op1, after, done):
                for s_, v in after:
                    dve.wait_ge(s_, v)
                if s2 is None:
                    nc.vector.tensor_scalar(dst, a, s1, None, op0).then_inc(*done)
                else:
                    nc.vector.tensor_scalar(dst, a, s1, s2, op0, op1).then_inc(*done)

            def stt(dst, a, s1, b, op0, op1, after, done):
                for s_, v in after:
                    dve.wait_ge(s_, v)
                nc.vector.scalar_tensor_tensor(out=dst, in0=a, scalar=s1, in1=b, op0=op0, op1=op1).then_inc(*done)

            def absolute(buf, x_):
                link(nc.vector.tensor_scalar(buf[:, 1, :], x_, -1.0, None, ALU.mult))
                link(nc.vector.tensor_tensor(buf[:, 2, :], x_, buf[:, 1, :], ALU.max))

            def artanh_argument(buf):
                link(nc.vector.tensor_scalar(buf[:, 4, :], buf[:, 3, :], 2.0, None, ALU.add))
                link(nc.vector.reciprocal(buf[:, 5, :], buf[:, 4, :]))
                link(nc.vector.tensor_tensor(buf[:, 4, :], buf[:, 3, :], buf[:, 5, :], ALU.mult))

            nc.vector.memset(rx[:, :], 0.0).then_inc(tile_summed, 2)
            link(nc.vector.memset(eps[:, :], EPS))
            link(nc.vector.memset(ones[:, :], 1.0))
            link(nc.vector.memset(pool_x[:, :, 0:16], 0.0))
            nc.vector.memset(total_g[:, :], 0.0).then_inc(odd_added, 1)
            dve.wait_ge(columns_landed, 16)
            absolute(ls, cols[:, COL["lam"]:COL["lam"] + 8])
            dve.wait_ge(scalar_chain, 1)
            artanh_argument(ls)
            assert chain[0] == LS_STEPS
            vector_split(dve, "rnn", 0, 0, ahead=0)
            for k in range(4):
                for c in range(4 * k, 4 * k + 4):
                    h_low(dve, norms["mix1"], c // 2, c % 2, col("g_mix", c))
                if k > 1:
                    vector_split(dve, "rnn", 0, k - 1, ahead=0)
            for k in range(KD // 2):
                dve.wait_ge(norms["mix1"].squared, 2 * k + 2)
                dve.wait_ge(odd_added, k + 1)
                nc.vector.tensor_tensor(total_g[:, :], total_g[:, :], four_squares(2 * k + 1), ALU.add)\
                    .then_inc(odd_added, 1)
                if k == 1:
                    vector_split(dve, "rnn", 0, 3, ahead=0)
            nc.vector.tensor_tensor(g_both[:, :], cols[:, COL["g_final"]:COL["g_final"] + KD],
                                    cols[:, COL["pre_mix"]:COL["pre_mix"] + KD], ALU.mult).then_inc(g_both_ready, 1)

            def recurrence(i, first):
                dp, dt = i * 8, i * 4
                V = lambda name: (rnn_v.sem, rnn_v.at(name, i))
                split("rnn", dp, 0)
                if first:
                    vsum("rnn", dt, 0, tsum[:, 0, :])
                    split("rnn", dp, 1)
                    norm_rstd(dve, norms["mix1"])
                    dve.wait_ge(norms["mix1"].rstd, 1)
                    vector_scale(dve, "rnn", dt, 0, rx[:, 3:3 + T], tsum[:, 0, :])
                else:
                    vscaled("rnn", dt, 0, tsum[:, 0, :], rx[:, 3:3 + T])
                    split("rnn", dp, 1)
                ts(u[:, :], rx[:, 0:T], col("conv0", i), col("conv_b", i), ALU.mult, ALU.add,
                   [(tile_scaled, scaled("rnn", dt, 0))], rnn_v.done("conv0"))
                for k, (before, name) in enumerate((("conv0", "conv1"), ("conv1", "conv2"), ("conv2", "u")), 1):
                    stt(u[:, :], rx[:, k:k + T], col(f"conv{k}", i), u[:, :], ALU.mult, ALU.add,
                        [V(before)], rnn_v.done(name))
                split("rnn", dp, 2)
                vscaled("rnn", dt, 1, tsum[:, 1, :], ry[:, :])
                split("rnn", dp, 3)
                split("rnn", dp, 4)
                stt(inner[:, :], y3[:, :], 0.044715, ry[:, :], ALU.mult, ALU.add,
                    [(rnn_g.sem, rnn_g.at("y3", i))], rnn_v.done("inner"))
                vscaled("rnn", dt, 2, tsum[:, 0, :])
                split("rnn", dp, 5)
                stt(gap[:, :], a2[:, :], 1.0, th[:, :], ALU.add, ALU.mult,
                    [(rnn_g.sem, rnn_g.at("a2", i)), (rnn_a.sem, rnn_a.at("th", i))], rnn_v.done("gap"))
                split("rnn", dp, 6)
                vscaled("rnn", dt, 3, tsum[:, 1, :])
                split("rnn", dp, 7)
                dve.wait_ge(rnn_g.sem, rnn_g.at("b_in", i))
                nc.vector.tensor_tensor_scan(hid[:, :], a_t[:, :], b_in[:, :], 0.0, ALU.mult, ALU.add)\
                    .then_inc(*rnn_v.done("hid"))
                tt(y_r[:, :], gl[:, :], hid[:, :], ALU.mult, [V("hid")], rnn_v.done("y"))
                tt(y[:, i, T:2 * T], y_r[:, :], y[:, i, 0:T].bitcast(F32), ALU.subtract,
                   [(rnn_a.sem, rnn_a.at("high", i))], rnn_v.done("low"))

            recurrence(0, True)
            with nc.vector.Fori(1, 8) as i:
                recurrence(i, False)

            split("forget", 0, 0)
            vscaled("forget", 0, 0, fl[:, :])
            split("forget", 0, 1)
            dve.wait_ge(tile_scaled, scaled("forget", 0, 0))
            link(nc.vector.tensor_scalar(lf[:, 0, :], fl[:, :], cols[:, COL["b_forget"]:COL["b_forget"] + 1],
                                         None, ALU.add))
            absolute(lf, lf[:, 0, :])

            def branch(stage, gates):
                muls = branch_mul[stage]
                first = stage == "rnn_branch"
                dve.wait_ge(gates_done[gates], 16)

                def tiles(i):
                    for t in range(4):
                        vsum(stage, i * 4, t, tsum[:, t % 2, :])
                        if stage != "pool_branch":
                            split(stage, i * 4, t)
                        o = i * 4 + t
                        dst = merged[:, o, :] if first else tmp[:, t % 2, :]
                        tt(dst, gate[:, o, :], tsum[:, t % 2, :], ALU.mult,
                           [(tile_summed, summed(stage, i * 4, t))], (muls, 1))
                        if stage == "pool_branch":
                            split(stage, i * 4, t)
                            dve.wait_ge(merged_high, i * 4 + (t + 1))
                            nc.vector.tensor_tensor(merged_hl[:, o, T:2 * T], merged[:, o, :],
                                                    merged_hl[:, o, 0:T].bitcast(F32), ALU.subtract)\
                                .then_inc(merged_low, 1)
                        elif not first:
                            tt(merged[:, o, :], merged[:, o, :], tmp[:, t % 2, :], ALU.add,
                               [(muls, i * 8 + (2 * t + 1))], (muls, 1))

                tiles(0)
                if first:
                    dve.wait_ge(scalar_chain, 2)
                    artanh_argument(lf)
                with nc.vector.Fori(1, 3) as i:
                    tiles(i)
                if first:
                    dve.wait_ge(forget_log, LOG_SIGMOID_STEPS)
                    link(nc.vector.memset(lf[:, 0, :], 1.0))
                    link(nc.vector.tensor_tensor_scan(fcum[:, :], lf[:, 0, :], lf[:, 7, :], 0.0, ALU.mult, ALU.add))
                    assert chain[0] == F_STEPS
                tiles(3)

            branch("rnn_branch", "rnn")
            dve.wait_ge(forget_p.sem, forget_p.at("FT"))
            link(nc.vector.tensor_copy(f_t[:, :, :], psV[:, 0:2 * P].rearrange("p (b q) -> p b q", b=2)))

            with nc.vector.Fori(0, 8) as i:
                dp, dt = i * 12, i * 6
                V = lambda name: (att_v.sem, att_v.at(name, i))
                split("attn", dp, 0)
                vscaled("attn", dt, 0, qT[:, :])
                split("attn", dp, 1)
                ts(fsel[:, :], fcum[:, :], ident[:, ds(i, 1)], None, ALU.mult, None, [(unit_landed, 16)],
                   att_v.done("fsel"))
                split("attn", dp, 2)
                vscaled("attn", dt, 1, kT[:, :])
                split("attn", dp, 3)
                split("attn", dp, 4)
                vscaled("attn", dt, 2, vT[:, :])
                split("attn", dp, 5)
                split("attn", dp, 6)
                stt(sc[:, :, :], psS[:, :, :], SCALE, biasm[:, :, :], ALU.mult, ALU.add,
                    [(att_p.sem, att_p.at("scores", i)), (att_g.sem, att_g.at("biasm", i))], att_v.done("s"))
                dve.wait_ge(*V("s"))
                nc.vector.tensor_reduce(st[:, 0:2], sc[:, :, :], AX.X, ALU.max).then_inc(*att_v.done("max"))
                ts(st[:, 2:4], st[:, 0:2], -1.0, None, ALU.mult, None, [V("max")], att_v.done("nmax"))
                vscaled("attn", dt, 3, tsum[:, 1, :], pool_x[:, i, 16:PADT])
                split("attn", dp, 7)
                dve.wait_ge(att_a.sem, att_a.at("e1", i))
                nc.vector.reciprocal(st[:, 6:8], st[:, 4:6]).then_inc(*att_v.done("recip"))
                for b in range(2):
                    ts(pr[:, b, :], pr[:, b, :], st[:, 6 + b:7 + b], None, ALU.mult, None, [V("recip")],
                       att_v.done(f"p{b}"))
                split("attn", dp, 8)
                dve.wait_ge(att_p.sem, att_p.at("vT", i))
                nc.vector.tensor_copy(vtok[:, :, :], psV[:, 0:2 * P].rearrange("p (b q) -> p b q", b=2))\
                    .then_inc(*att_v.done("vtok"))
                vscaled("attn", dt, 4, tsum[:, 0, :])
                split("attn", dp, 9)
                split("attn", dp, 10)
                vscaled("attn", dt, 5, tsum[:, 1, :])
                split("attn", dp, 11)
                tt(y[:, i, T:2 * T], psO[:, 0:T], y[:, i, 0:T].bitcast(F32), ALU.subtract,
                   [(att_a.sem, att_a.at("high", i))], att_v.done("low"))
            dve.wait_ge(tile_scaled, scaled("attn", 42, 5))
            nc.vector.memset(tmp[:, 1, 0:1], 0.0).then_inc(poolx_pad, 1)
            branch("attn_branch", "attn")

            def pool_gates(i):
                for b in range(2):
                    split("pool", i * 4, 2 * b)
                    vscaled("pool", i * 2, b, tsum[:, b, :])
                    split("pool", i * 4, 2 * b + 1)

            with nc.vector.Fori(0, POOLED_AFTER) as i:
                pool_gates(i)
            for c in range(8):
                tt(y[:, c, T:2 * T], tmp[:, c % 2, :], y[:, c, 0:T].bitcast(F32), ALU.subtract,
                   [(pool_a.sem, pool_a.at(f"h{c}"))], pool_v.done(f"l{c}"))
            with nc.vector.Fori(POOLED_AFTER, 8) as i:
                pool_gates(i)
            branch("pool_branch", "pool")

            with nc.vector.Fori(0, 8) as i:
                for b in range(2):
                    split("out", i * 4, 2 * b)
                    vsum("out", i * 2, b, tsum[:, b, :])
                    tt(x[:, i * 2 + b, :], x[:, i * 2 + b, :], tsum[:, b, :], ALU.add,
                       [(tile_summed, summed("out", i * 2, b))], (x_added, 1))
                    split("out", i * 4, 2 * b + 1)
                    h_low(dve, norms["ffn1"], i, b, col("g_ffn", i * 2 + b))
            norm_rstd(dve, norms["ffn1"])
            with nc.vector.Fori(0, KF) as i:
                dp, dt = i * 4, i * 2
                split("up", dp, 0)
                vscaled("up", dt, 0, tsum[:, 0, :])
                split("up", dp, 1)
                split("up", dp, 2)
                vscaled("up", dt, 1, tsum[:, 1, :])
                tt(tmp[:, 0, :], tmp[:, 1, :], tsum[:, 1, :], ALU.mult,
                   [(up_a.sem, up_a.at("silu", i)), (tile_scaled, scaled("up", dt, 1))], up_v.done("prod"))
                split("up", dp, 3)
                tt(hidden[:, i, T:2 * T], tmp[:, 0, :], hidden[:, i, 0:T].bitcast(F32), ALU.subtract,
                   [(up_a.sem, up_a.at("high", i))], up_v.done("low"))
            with nc.vector.Fori(0, 2) as i:
                for k in range(KF):
                    for t in DOWN_ENDS.get(k, []):
                        vsum("down", i * 8, t, tsum[:, t % 2, :])
                        tt(x[:, i * 8 + t, :], x[:, i * 8 + t, :], tsum[:, t % 2, :], ALU.add,
                           [(tile_summed, summed("down", i * 8, t))], (down_x, 1))
                    split("down", i * KF, k)
                    for t in DOWN_ENDS.get(k, []):
                        h_low(dve, norms["mix2"], i * 4 + t // 2, t % 2, g_both[:, ds(i * 8 + t, 1)])
            dve.wait_ge(norms["mix2"].sums, 1)
            ts(tmp[:, 0, :], psN[:, 0:T], EPS / D, EPS * EPS, ALU.mult, ALU.add, [], (squared_mix, 1))
            stt(tmp[:, 1, :], psN[:, T:2 * T], 1.0 / D, tmp[:, 0, :], ALU.mult, ALU.add, [(squared_mix, 1)],
                (squared_mix, 1))
            norm_rstd(dve, norms["mix2"])
            dve.wait_ge(norms["mix2"].rstd, 1)


            def rope(steps, scal, tens, g, i, dst, name):
                W = lambda s: (steps.sem, steps.at(s, i))
                dve.wait_ge(scal.sem, scal.at("root", i))
                nc.vector.reciprocal(rrs[:, :], root[:, :]).then_inc(*steps.done("rstd"))
                tt(rcos[:, :], rg[:, :], cos_t[:, :], ALU.mult, [], steps.done("cos"))
                tt(rsin[:, :], psN[:, T:2 * T], sin_t[:, :], ALU.mult, [], steps.done("sin"))
                tt(rsum[:, :], rcos[:, :], rsin[:, :], ALU.add, [W("sin")], steps.done("sum"))
                tt(dst, rsum[:, :], rrs[:, :], ALU.mult, [W("sum")], steps.done(name))

            def tail_tok(m):
                dve.wait_ge(tail_p.sem, tail_p.at("vT", m))
                nc.vector.tensor_copy(vb_tok[:, :, :], psV[:, 0:2 * P].rearrange("p (b q) -> p b q", b=2))\
                    .then_inc(*tail_v.done("vtok"))

            def tail_low(m):
                tt(mixed[:, m + 8, T:2 * T], psO[:, T:2 * T], mixed[:, m + 8, 0:T].bitcast(F32), ALU.subtract,
                   [(tail_a.sem, tail_a.at("high", m))], tail_v.done("low"))

            def heads(m, dp, dt, tail):
                V = lambda name: (b2_v.sem, b2_v.at(name, m))
                if tail:
                    tail_tok(m - 1)
                split("mix", dp, 4)
                vscaled("mix", dt, 2, rv[:, :])
                ts(rg[:, :], rv[:, :], cols[:, COL["q_norm"]:COL["q_norm"] + 1], None, ALU.mult, None,
                   [(tile_scaled, scaled("mix", dt, 2))], b2_v.done("g"))
                split("mix", dp, 5)
                if tail:
                    tail_low(m - 1)
                split("mix", dp, 6)
                rope(b2_v, b2_a, b2_p, "q_norm", m, q_r[:, :], "q")
                vscaled("mix", dt, 3, kb[:, :])
                split("mix", dp, 7)
                split("mix", dp, 8)
                dve.wait_ge(b2_p.sem, b2_p.at("scoresA", m))
                nc.vector.tensor_reduce(stA[:, 0:2], psS[:, :, :], AX.X, ALU.max).then_inc(*b2_v.done("maxA"))
                ts(stA[:, 2:4], stA[:, 0:2], -SCALE, None, ALU.mult, None, [V("maxA")], b2_v.done("nmaxA"))
                vscaled("mix", dt, 4, qb[:, :])
                dve.wait_ge(b2_a.sem, b2_a.at("e1A", m))
                nc.vector.reciprocal(stA[:, 6:8], stA[:, 4:6]).then_inc(*b2_v.done("recipA"))
                for b in range(2):
                    ts(pA[:, b, :], pA[:, b, :], stA[:, 6 + b:7 + b], None, ALU.mult, None, [V("recipA")],
                       b2_v.done(f"p{b}A"))
                split("mix", dp, 9)
                stt(sB[:, :, :], psF[:, :, :], SCALE, rbm[:, :, :], ALU.mult, ALU.add,
                    [(b2_p.sem, b2_p.at("scoresB", m)), (b2_g.sem, b2_g.at("rbm", m))], b2_v.done("sB"))
                dve.wait_ge(*V("sB"))
                nc.vector.tensor_reduce(stB[:, 0:2], sB[:, :, :], AX.X, ALU.max).then_inc(*b2_v.done("maxB"))
                ts(stB[:, 2:4], stB[:, 0:2], -1.0, None, ALU.mult, None, [V("maxB")], b2_v.done("nmaxB"))
                split("mix", dp, 10)
                dve.wait_ge(b2_a.sem, b2_a.at("e1B", m))
                nc.vector.reciprocal(stB[:, 6:8], stB[:, 4:6]).then_inc(*b2_v.done("recipB"))
                for b in range(2):
                    ts(pB[:, b, :], pB[:, b, :], stB[:, 6 + b:7 + b], None, ALU.mult, None, [V("recipB")],
                       b2_v.done(f"p{b}B"))
                vscaled("mix", dt, 5, vb[:, :])
                tt(mixed[:, m, T:2 * T], psO[:, 0:T], mixed[:, m, 0:T].bitcast(F32), ALU.subtract,
                   [(b2_a.sem, b2_a.at("highA", m))], b2_v.done("lowA"))
                split("mix", dp, 11)
                for b in range(2):
                    c = m * 2 + b
                    stt(x[:, c, :], x[:, c, :], col("g_final", c), rstd_x[:, :], ALU.mult, ALU.mult,
                        [], (x_final, 1))

            for j in range(2):
                dp = j * 36
                split("mix", dp, 0)
                vscaled("mix", j * 18, 0, rv[:, :])
                split("mix", dp, 1)
                if j == 0:
                    dve.wait_ge(norms["final"].root, 1)
                    nc.vector.reciprocal(rstd_x[:, :], tmp[:, 0, :]).then_inc(norms["final"].rstd, 1)
                ts(rg[:, :], rv[:, :], cols[:, COL["k_norm"]:COL["k_norm"] + 1], None, ALU.mult, None,
                   [(tile_scaled, scaled("mix", j * 18, 0))], kv_v.done("g"))
                split("mix", dp, 2)
                vscaled("mix", j * 18, 1, va[:, :])
                split("mix", dp, 3)
                dve.wait_ge(const4_landed, 64)
                rope(kv_v, kv_a, kv_p, "k_norm", j, k_r[:, :], "k")
                dve.wait_ge(kv_p.sem, kv_p.at("v", j))
                nc.vector.tensor_copy(va_tok[:, :, :], psV[:, 0:2 * P].rearrange("p (b q) -> p b q", b=2))\
                    .then_inc(*kv_v.done("vtok"))
                if j == 0:
                    heads(0, 0, 0, False)
                with nc.vector.Fori(1 - j, 4) as i:
                    heads(i + j * 4, i * 8 + j * 36, i * 4 + j * 18, True)
            tail_tok(7)
            tail_low(7)

            with nc.vector.Fori(0, 8) as i:
                for b in range(2):
                    split("wo", i * 4, 2 * b)
                    vsum("wo", i * 2, b, tsum[:, b, :])
                    split("wo", i * 4, 2 * b + 1)

            def updated(n, before, src, scaled_before, g, added):
                def add(c):
                    tt(x[:, c, :], x[:, c, :], src[:, c, :], ALU.add, [(post_scaled, scaled_before + c + 1)],
                       (added, 1))

                early = 0 if n is norms["mlp2"] else EARLY
                if not early:
                    norm_rstd(dve, before, rstd_x)
                    dve.wait_ge(x_final, KD)
                add(early)
                add(early + 1)
                for c in range(max(early - 2, 0), KD):
                    h_low(dve, n, 0, c, col(g, c))
                    if early <= c < KD - 2:
                        add(c + 2)
                norm_rstd(dve, n)

            updated(norms["mlp2"], norms["mixed2"], mix32, 0, "pre_mlp", x_mixed)
            dve.wait_ge(acc_zero, 1)
            for j in range(2):
                if j == 1:
                    tt(p_hl[:, :, T:2 * T], p_raw[:, :, :], p_hl[:, :, 0:T].bitcast(F32), ALU.subtract,
                       [(p_split, 1)], (p_split, 1))
                with nc.vector.Fori(0, 16) as i:
                    dp, dt = j * 128 + i * 4, j * 48 + i * 2
                    for b in range(2):
                        m = j * 32 + i * 2 + b
                        split("mlp", dp, 2 * b)
                        vscaled("mlp", dt, b, tsum[:, b, :])
                        stt(tmp[:, b, :], tsum[:, b, :], 0.0, tsum[:, b, :], ALU.max, ALU.mult,
                            [(tile_scaled, scaled("mlp", j * 32 + i * 2, b))], sq_v.done("sq"))
                        split("mlp", dp, 2 * b + 1)
                        tt(hidden2[:, i * 2 + b, T:2 * T], tmp[:, b, :], hidden2[:, i * 2 + b, 0:T].bitcast(F32),
                           ALU.subtract, [(sq_a.sem, sq_a.at("high", m))], sq_v.done("low"))
                with nc.vector.Fori(0, 8) as i:
                    dp, dt = j * 128 + i * 8, j * 48 + i * 2
                    for k in range(8):
                        if k % 4 == 3:
                            b = k // 4
                            vsum("mlp", dt, 32 + b, tsum[:, b, :])
                            tt(acc[:, i * 2 + b, :], acc[:, i * 2 + b, :], tsum[:, b, :], ALU.add,
                               [(tile_summed, summed("mlp", dt, 32 + b))], (acc_added, 1))
                        split("mlp", dp, 64 + k)
            for t in range(16):
                vsum("ple", 0, t, e[:, t, :])
                if t == 5:
                    norm_rstd(dve, norms["mlped2"], rstd_x)
                if t % 4 == 3:
                    split("ple", 0, t // 4)
                if t >= KD - EARLY:
                    c = t - (KD - EARLY)
                    tt(x[:, c, :], x[:, c, :], acc[:, c, :], ALU.add, [(post_scaled, KD + c + 1)], (x_mlped, 1))
                    if c > 1:
                        h_low(dve, norms["ple2"], 0, c - 2, col("pre_ple", c - 2))
            updated(norms["ple2"], norms["mlped2"], acc, KD, "pre_ple", x_mlped)

            def embed(i, last):
                for b in range(2):
                    if not last:
                        split("ple_gate", i * 4, 2 * b)
                    vscaled("ple_gate", i * 2, b, tsum[:, b, :])
                    if not last:
                        split("ple_gate", i * 4, 2 * b + 1)
                    tt(e[:, i * 2 + b, :], e[:, i * 2 + b, :], tmp[:, b, :], ALU.mult,
                       [(ple_a, i * 2 + (b + 1))], (ple_v, 1))

            with nc.vector.Fori(0, 7) as i:
                embed(i, False)
            embed(7, True)
            norm_rstd(dve, norms["pled2"], rstd_x)
            dve.wait_ge(norms["pled2"].rstd, 1)
            dve.wait_ge(e_gained, KD)
            def scale_e(c):
                tt(e[:, c, :], e[:, c, :], rstd_x[:, :], ALU.mult, [], (result_t, 1))

            scale_e(0)
            for c in range(RESULT_V):
                if c + 1 < RESULT_V:
                    scale_e(c + 1)
                tt(x[:, c, :], x[:, c, :], e[:, c, :], ALU.add, [(result_t, c + 1)], (result_v, 1))

        @block.tensor
        def _(pe):
            mm = nc.tensor.matmul

            def tile(stage, dp, dt, t, first_piece, rhs, chunks=KD, norm=None, between=None, ready=None):
                tile_matmuls(pe, stage, dp, dt, t, first_piece * BLOCKS, chunks, rhs, norm, between=between,
                             ready=ready)

            def transposed(dst, src):
                return nc.tensor.transpose(dst, src, ident[:, :])

            pe.wait_ge(vector_chain, 2)

            def recurrence(i, first):
                dp, dt = i * 8, i * 4

                def gates():
                    pe.wait_ge(wgate_landed, i * 16 + 16)
                    pe.wait_ge(rnn_v.sem, rnn_v.at("u", i))
                    mm(psS[:, 0, :], wgate[:, 0:P], u[:, :], start=True, stop=True)
                    mm(psS[:, 1, :], wgate[:, P:2 * P], u[:, :], start=True, stop=True)\
                        .then_inc(*rnn_p.done("gates"))

                tile("rnn", dp, dt, 0, 0, h_chunk, norm=norms["mix1"] if first else None)
                tile("rnn", dp, dt, 1, 2, h_chunk)
                if first:
                    pe.wait_ge(even_added, KD // 2 + 1)
                    mm(psN[:, 0:T], ones[:, :], total[:, :], start=True, stop=False)
                    pe.wait_ge(odd_added, KD // 2 + 1)
                    mm(psN[:, 0:T], ones[:, :], total_g[:, :], start=False, stop=True)\
                        .then_inc(norms["mix1"].sums, 1)
                tile("rnn", dp, dt, 2, 4, h_chunk, between=None if first else {GATES_AT: gates})
                tile("rnn", dp, dt, 3, 6, h_chunk, between={2: gates} if first else None)

            recurrence(0, True)
            with nc.tensor.Fori(1, 8) as i:
                recurrence(i, False)
            tile("forget", 0, 0, 0, 0, h_chunk)

            def branch_tiles(stage, i, between=((), ())):
                for t in range(4):
                    tile(stage, i * 4, i * 4, t, t, y_chunk, chunks=8, between=between[1] if t == between[0] else None)

            def forget_transposed():
                pe.wait_ge(unit_landed, 16)
                pe.wait_ge(vector_chain, F_STEPS)
                for b in range(2):
                    last = transposed(psV[:, b * P:(b + 1) * P], fcum[:, b * P:(b + 1) * P])
                last.then_inc(*forget_p.done("FT"))

            def branch(stage, ready, before):
                pe.wait_ge(*before)
                branch_tiles(stage, 0, (0, {7: lambda: pe.wait_ge(*ready)}))
                with nc.tensor.Fori(1, 3) as i:
                    branch_tiles(stage, i)
                if stage == "rnn_branch":
                    branch_tiles(stage, 3, (2, {4: forget_transposed}))
                else:
                    branch_tiles(stage, 3)

            branch("rnn_branch", (rnn_v.sem, rnn_v.at("low", 7)), (rnn_v.sem, rnn_v.at("low", 6)))

            with nc.tensor.Fori(0, 8) as i:
                dp, dt = i * 12, i * 6
                for t in range(3):
                    tile("attn", dp, dt, t, 2 * t, h_chunk)
                pe.wait_ge(tile_scaled, scaled("attn", dt, 1))
                for b in range(2):
                    last = mm(psS[:, b, :], qT[:, b * P:(b + 1) * P], kT[:, :], start=True, stop=True)
                last.then_inc(*att_p.done("scores"))
                pe.wait_ge(att_v.sem, att_v.at("fsel", i))
                mm(psF[:, 0, :], ones[:, :], fsel[:, :], start=True, stop=True).then_inc(*att_p.done("fk"))
                tile("attn", dp, dt, 3, 6, h_chunk)
                pe.wait_ge(tile_scaled, scaled("attn", dt, 2))
                for b in range(2):
                    last = transposed(psV[:, b * P:(b + 1) * P], vT[:, b * P:(b + 1) * P])
                last.then_inc(*att_p.done("vT"))
                tile("attn", dp, dt, 4, 8, h_chunk)
                pe.wait_ge(att_v.sem, att_v.at("p1", i))
                for b in range(2):
                    for kb_ in range(2):
                        last = transposed(psT[:, kb_, b * P:(b + 1) * P], pr[:, b, kb_ * P:(kb_ + 1) * P])
                last.then_inc(*att_p.done("pT"))
                tile("attn", dp, dt, 5, 10, h_chunk)
                pe.wait_ge(att_a.sem, att_a.at("prT", i))
                pe.wait_ge(att_v.sem, att_v.at("vtok", i))
                for b in range(2):
                    last = mm(psO[:, 0:T], vtok[:, b, :], prT[:, b, :], start=b == 0, stop=b == 1)
                last.then_inc(*att_p.done("out"))
            branch("attn_branch", (att_v.sem, att_v.at("low", 7)), (att_v.sem, att_v.at("low", 6)))

            with nc.tensor.Fori(0, POOLED_AFTER) as i:
                for b in range(2):
                    tile("pool", i * 4, i * 2, b, 2 * b, h_chunk)
            pe.wait_ge(const3_landed, 32)
            for g in range(4):
                pe.wait_ge(pooled_done, POOLED[g])
                if g == 3:
                    pe.wait_ge(pool_a.sem, pool_a.at("s1"))
                bank = (psS, psF, psT)[g % 3]
                for m in range(2):
                    for c in range(2):
                        last = mm(bank[:, m, :], wpool[:, g, c, m * P:(m + 1) * P], pooled[:, 2 * g + c, :],
                                  start=c == 0, stop=c == 1)
                last.then_inc(*pool_p.done(f"y{g}"))
            with nc.tensor.Fori(POOLED_AFTER, 8) as i:
                for b in range(2):
                    tile("pool", i * 4, i * 2, b, 2 * b, h_chunk)
            branch("pool_branch", (pool_v.sem, pool_v.at("l7")), (pool_v.sem, pool_v.at("l6")))

            tile("out", 0, 0, 0, 0, merged_chunk, ready=merged_low)
            tile("out", 0, 0, 1, 2, merged_chunk)
            with nc.tensor.Fori(1, 8) as i:
                for b in range(2):
                    tile("out", i * 4, i * 2, b, 2 * b, merged_chunk)
            tile("up", 0, 0, 0, 0, h_chunk, norm=norms["ffn1"])
            norm_tensor(pe, norms["ffn1"])
            tile("up", 0, 0, 1, 2, h_chunk)
            with nc.tensor.Fori(1, KF) as i:
                for b in range(2):
                    tile("up", i * 4, i * 2, b, 2 * b, h_chunk)
            pe.wait_ge(up_v.sem, up_v.at("low", KF - 2))

            def last_hidden():
                pe.wait_ge(up_v.sem, up_v.at("low", KF - 1))

            with nc.tensor.Fori(0, 2) as i:
                for t in range(8):
                    tile_matmuls(pe, "down", i * KF, i * 8, t, t * KF, KF, lambda c: hidden[:, c, :],
                                 between=None if t else {KF - 1: last_hidden})
            def turned(square, steps):
                pe.wait_ge(*square)
                mm(psN[:, 0:T], ones[:, :], rsq[:, :], start=True, stop=True).then_inc(*steps.done("stat"))

            def block1_norms():
                total_tensor(pe, norms["final"], total, 0)
                total_tensor(pe, norms["mix2"], total_g, 1)

            def tail(m, kv):
                def probabilities():
                    pe.wait_ge(b2_v.sem, b2_v.at("p1B", m))
                    for b in range(2):
                        for kb_ in range(2):
                            last = transposed(psS[:, kb_, b * P:(b + 1) * P], pB[:, b, kb_ * P:(kb_ + 1) * P])
                    last.then_inc(*tail_p.done("pT"))

                def values():
                    pe.wait_ge(b2_v.sem, b2_v.at("lowA", m))
                    pe.wait_ge(kv_v.sem, kv_v.at("vtok", kv))
                    for b in range(2):
                        last = transposed(psV[:, b * P:(b + 1) * P], vb[:, b * P:(b + 1) * P])
                    last.then_inc(*tail_p.done("vT"))

                def product():
                    pe.wait_ge(tail_a.sem, tail_a.at("pT", m))
                    pe.wait_ge(tail_v.sem, tail_v.at("vtok", m))
                    for b in range(2):
                        last = mm(psO[:, T:2 * T], vb_tok[:, b, :], pBT[:, b, :], start=b == 0, stop=b == 1)
                    last.then_inc(*tail_p.done("out"))

                return probabilities, values, product

            def heads(j, m, dp, dt, with_tail, first=None):
                def stat_and_turn():
                    turned((b2_a.sem, b2_a.at("square", m)), b2_p)
                    pe.wait_ge(b2_v.sem, b2_v.at("g", m))
                    mm(psN[:, T:2 * T], turn[:, :], rg[:, :], start=True, stop=True)\
                        .then_inc(*b2_p.done("turn"))

                def scores_a():
                    pe.wait_ge(b2_v.sem, b2_v.at("q", m))
                    for b in range(2):
                        last = mm(psS[:, b, :], q_r[:, b * P:(b + 1) * P], k_r[:, :], start=True, stop=True)
                    last.then_inc(*b2_p.done("scoresA"))

                def scores_b():
                    pe.wait_ge(tile_scaled, scaled("mix", dt, 4))
                    for b in range(2):
                        last = mm(psF[:, b, :], qb[:, b * P:(b + 1) * P], kb[:, :], start=True, stop=True)
                    last.then_inc(*b2_p.done("scoresB"))

                def probabilities_a():
                    pe.wait_ge(b2_v.sem, b2_v.at("p1A", m))
                    for b in range(2):
                        for kb_ in range(2):
                            last = transposed(psT[:, kb_, b * P:(b + 1) * P], pA[:, b, kb_ * P:(kb_ + 1) * P])
                    last.then_inc(*b2_p.done("pTA"))

                if with_tail:
                    probabilities, values, product = tail(m - 1, j)
                    tile("mix", dp, dt, 2, 4, h_chunk, between={7: probabilities, 11: values})
                    tile("mix", dp, dt, 3, 6, h_chunk, between={2: product, 10: stat_and_turn})
                else:
                    tile("mix", dp, dt, 2, 4, h_chunk, between=first)
                    tile("mix", dp, dt, 3, 6, h_chunk, between={10: stat_and_turn})
                tile("mix", dp, dt, 4, 8, h_chunk, between={12: scores_a})
                tile("mix", dp, dt, 5, 10, h_chunk, between={9: scores_b, 12: probabilities_a})
                pe.wait_ge(b2_a.sem, b2_a.at("pAT", m))
                for b in range(2):
                    last = mm(psO[:, 0:T], va_tok[:, b, :], pAT[:, b, :], start=b == 0, stop=b == 1)
                last.then_inc(*b2_p.done("outA"))

            for j in range(2):
                if j == 0:
                    tile("mix", 0, 0, 0, 0, h_chunk, norm=norms["mix2"])
                    block1_norms()
                else:
                    tile("mix", j * 36, j * 18, 0, 0, h_chunk)
                tile("mix", j * 36, j * 18, 1, 2, h_chunk)

                def key_turned():
                    pe.wait_ge(const4_landed, 64)
                    turned((kv_a.sem, kv_a.at("square", j)), kv_p)
                    pe.wait_ge(kv_v.sem, kv_v.at("g", j))
                    mm(psN[:, T:2 * T], turn[:, :], rg[:, :], start=True, stop=True).then_inc(*kv_p.done("turn"))

                def value_transposed():
                    pe.wait_ge(tile_scaled, scaled("mix", j * 18, 1))
                    for b in range(2):
                        last = transposed(psV[:, b * P:(b + 1) * P], va[:, b * P:(b + 1) * P])
                    last.then_inc(*kv_p.done("v"))

                if j == 0:
                    heads(0, 0, 0, 0, None, {6: key_turned, 10: value_transposed})
                else:
                    key_turned()
                    value_transposed()
                with nc.tensor.Fori(1 - j, 4) as i:
                    heads(j, i + j * 4, i * 8 + j * 36, i * 4 + j * 18, True)
            probabilities, values, product = tail(7, 1)

            def last_mixed():
                pe.wait_ge(tail_v.sem, tail_v.at("low", 7))

            def last_global():
                pe.wait_ge(b2_v.sem, b2_v.at("lowA", 7))

            pe.wait_ge(tail_v.sem, tail_v.at("low", 6))
            tile("wo", 0, 0, 0, 0, lambda c: mixed[:, c, :],
                 between={6: probabilities, 7: last_global, 10: values, 14: product, 15: last_mixed})
            tile("wo", 0, 0, 1, 2, lambda c: mixed[:, c, :])
            with nc.tensor.Fori(1, 8) as i:
                for b in range(2):
                    tile("wo", i * 4, i * 2, b, 2 * b, lambda c: mixed[:, c, :])
            norm_tensor(pe, norms["mixed2"])
            tile("mlp", 0, 0, 0, 0, h_chunk, norm=norms["mlp2"])
            tile("mlp", 0, 0, 1, 2, h_chunk)
            for j in range(2):
                with nc.tensor.Fori(1 - j, 16) as i:
                    for b in range(2):
                        tile("mlp", j * 128 + i * 4, j * 48 + i * 2, b, 2 * b, h_chunk)
                pe.wait_ge(sq_v.sem, sq_v.at("low", j * 32 + 30))

                def last_hidden():
                    pe.wait_ge(sq_v.sem, sq_v.at("low", j * 32 + 31))

                with nc.tensor.Fori(0, 8) as i:
                    for b in range(2):
                        tile("mlp", j * 128 + i * 8, j * 48 + i * 2, 32 + b, 64 + 4 * b,
                             lambda c: hidden2[:, c, :], chunks=32, between=None if b else {31: last_hidden})
            pe.wait_ge(p_split, 2)
            for t in range(16):
                tile_matmuls(pe, "ple", 0, 0, t, 2 * t, 2, lambda c: p_hl[:, c, :], tile_sem=ple_tile_done)
                if t == 3:
                    norm_tensor(pe, norms["mlped2"])
            tile("ple_gate", 0, 0, 0, 0, h_chunk, norm=norms["ple2"])
            tile("ple_gate", 0, 0, 1, 2, h_chunk)
            with nc.tensor.Fori(1, 8) as i:
                for b in range(2):
                    tile("ple_gate", i * 4, i * 2, b, 2 * b, h_chunk)
            norm_tensor(pe, norms["pled2"])


DOWN_ENDS = {}
for _t in range(8):
    DOWN_ENDS.setdefault(((_t + 1) * KF - 1) // BLOCKS, []).append(_t)

RESULT_V = 11

LOG_SIGMOID_STEPS = 2 + 8 * 2 + 4

LS_STEPS = 3 + 2 + 3
F_STEPS = LS_STEPS + 1 + 2 + 3 + 2
POOLED = [1 + sum(k + 1 + 3 for k in range(g + 1)) for g in range(4)]


def _stream(inputs):
    import numpy as np

    def blocks(m):
        k, o = m.shape
        return m.reshape(k // P, P, o // P, P).transpose(2, 0, 1, 3)

    W = {k: np.asarray(v)[0] for k, v in inputs.items() if k.startswith("w_")}
    w_in, out = W["w_in"], []

    def put(b):
        out.append(b.reshape(-1, P, P))

    o = 0
    where = {}
    for name, width in (("rx", 1024), ("ry", 1024), ("q", 1024), ("k", 1024), ("v", 1024), ("f", 8), ("pool", 1024),
                        ("gate", 6144)):
        where[name] = o
        o += width

    def part(name, tile):
        c = where[name] + tile * P
        return blocks(w_in[:, c:c + P])

    for i in range(8):
        put(part("rx", i)), put(part("ry", i)), put(part("gate", 2 * i)), put(part("gate", 2 * i + 1))
    put(part("f", 0))
    put(blocks(W["w_branch_rnn"]))
    for i in range(8):
        for name in ("q", "k", "v", "pool"):
            put(part(name, i))
        put(part("gate", 16 + 2 * i)), put(part("gate", 17 + 2 * i))
    put(blocks(W["w_branch_attn"]))
    for i in range(16):
        put(part("gate", 32 + i))
    put(blocks(W["w_branch_pool"]))
    put(blocks(W["w_out"]))
    gate_up = blocks(W["w_ffn_in"])
    for i in range(KF):
        put(gate_up[i]), put(gate_up[KF + i])
    put(blocks(W["w_ffn_out"]))
    in2 = blocks(W["w_in_2"])
    for j in range(2):
        put(in2[8 + j]), put(in2[10 + j])
        for i in range(4 * j, 4 * j + 4):
            put(in2[i]), put(in2[20 + i]), put(in2[12 + i]), put(in2[28 + i])
    put(blocks(W["w_o_2"]))
    up, down = blocks(W["w_up_2"]), blocks(W["w_down_2"])
    for half in range(2):
        put(up[32 * half:32 * half + 32]), put(down[:, 32 * half:32 * half + 32])
    put(blocks(W["w_ple_proj_2"])), put(blocks(W["w_ple_gate_2"]))
    flat = np.concatenate(out)
    assert len(flat) == PIECES * BLOCKS
    groups = -(-PIECES // RING)
    stream = np.empty((groups * RING, P, BLOCKS, P), flat.dtype)
    stream[:PIECES] = flat.reshape(PIECES, BLOCKS, P, P).transpose(0, 2, 1, 3)
    stream[PIECES:] = 0
    return stream.reshape(groups, RING, P, PIECE)


def _tables():
    import numpy as np
    far = np.float32(-1e30)
    q = np.arange(T)
    causal = np.where(q[:, None] >= q[None, :], np.float32(0), far)
    c = q % 64
    c0 = np.clip(c - 8, 0, 48)
    near = np.where((c[None, :] >= c0[:, None]) & (c[None, :] < c0[:, None] + 16), np.float32(0), far)

    def by_query(m):
        return np.ascontiguousarray(m.reshape(2, P, T).transpose(1, 0, 2))

    freqs = np.float32(10000.0) ** (-np.arange(32, dtype=np.float32) / 32)
    angle = np.empty((P, T), np.float32)
    turn = np.zeros((P, P), np.float32)
    for axis, pos in ((0, q // 64), (1, q % 64)):
        for half in range(2):
            d = 64 * axis + 32 * half
            angle[d:d + 32] = freqs[:, None] * pos.astype(np.float32)[None, :]
            for n in range(32):
                turn[64 * axis + 32 * (1 - half) + n, d + n] = 1.0 if half else -1.0
    inv = np.stack([1.0 / np.minimum(np.arange(1, T + 1), wdw) for wdw in (2, 4, 8, 16)]).astype(np.float32)
    return {
        "causal_mask": by_query(causal), "near_mask": by_query(near), "rope_cos": np.cos(angle),
        "rope_sin": np.sin(angle), "rope_turn": turn,
        "inv_count": np.ascontiguousarray(np.broadcast_to(inv, (P, 4, T))), "unit": np.eye(P, dtype=np.float32),
    }


def _arrays(inputs):
    import numpy as np
    A = {k: np.asarray(v) for k, v in inputs.items()}

    def chunks(v):
        return v.reshape(-1, P).T

    cols = np.zeros((P, NCOL), np.float32)
    for name, v in (("g_mix", A["g_mix"]), ("g_ffn", A["g_ffn"]), ("g_final", A["g_final"]),
                    ("pre_mix", A["pre_mix_norm_2"]), ("post_mix", A["post_mix_norm_2"]),
                    ("pre_mlp", A["pre_mlp_norm_2"]), ("post_mlp", A["post_mlp_norm_2"]),
                    ("pre_ple", A["pre_ple_norm_2"]), ("post_ple", A["post_ple_norm_2"]),
                    ("conv0", A["conv_w"][0, 0]), ("conv1", A["conv_w"][0, 1]), ("conv2", A["conv_w"][0, 2]),
                    ("conv3", A["conv_w"][0, 3]), ("conv_b", A["conv_b"]), ("b_rg", A["b_rg"]), ("b_ig", A["b_ig"]),
                    ("lam", A["lru_lambda"]), ("pool_scale", A["pool_scale"]), ("q_norm", A["q_norm_2"]),
                    ("k_norm", A["k_norm_2"])):
        c = chunks(v)
        cols[:, COL[name]:COL[name] + c.shape[1]] = c
    cols[:HEADS, COL["b_forget"]] = A["b_forget"][0]
    q = np.arange(T)
    row, column = q // 64, q % 64
    dr = row[None, :] - row[:, None] + 7
    dc = np.clip(column[None, :] - column[:, None] + 15, 0, 30)
    rel = A["rel_pos_bias_2"][0][:, dr, dc]
    return {
        "w": _stream(A),
        "xT": np.ascontiguousarray(A["x"][0].T.reshape(KD, P, T).transpose(1, 0, 2)),
        "pT": np.ascontiguousarray(A["p_2"][0, 0].T.reshape(2, P, T).transpose(1, 0, 2)),
        "columns": cols,
        "w_gates": np.ascontiguousarray(np.concatenate([A["w_rg"][0], A["w_ig"][0]], axis=2)),
        "w_pool": np.ascontiguousarray(A["w_pool"][0].reshape(4, 2, P, 2 * P).transpose(2, 0, 1, 3)),
        "rel_bias": np.ascontiguousarray(rel.reshape(HEADS, 2, P, T).transpose(0, 2, 1, 3)),
        **_tables(),
    }


_ORDER = ["w", "xT", "pT", "columns", "w_gates", "w_pool", "rel_bias", "near_mask", "causal_mask", "rope_cos",
          "rope_sin", "rope_turn", "inv_count", "unit"]


def kernel(**inputs):
    import numpy as np
    import concourse.bacc as _bacc
    from concourse import mybir as _mybir
    from concourse.bass_utils import run_bass_kernel_spmd as _run

    nc = _bacc.Bacc("TRN2", target_bir_lowering=False, num_devices=1)
    arrays = _arrays(inputs)
    args = [nc.dram_tensor(n, arrays[n].shape, _mybir.dt.from_np(arrays[n].dtype), kind="ExternalInput").ap()
            for n in _ORDER]
    out = nc.dram_tensor("outT", (P, KD, T), F32, kind="ExternalOutput").ap()
    build(nc, *args, out)
    r = _run(nc, [arrays], core_ids=[0])
    got = r.results[0]["outT"]
    return np.ascontiguousarray(np.asarray(got).transpose(2, 1, 0).reshape(1, T, D))
```
